# Optimizing a Trainium2 kernel written in Bass

```python
import jax, jax.numpy as jnp
from jax import lax
import numpy as np
import math
import jax
import jax.numpy as jnp

D_MODEL = 1024
BATCH = 1
SEQ = 256
DEPTH = 2

HEAD_DIM = 64
N_Q_HEADS = 8
N_KV_HEADS = 2
GQA_GROUP = N_Q_HEADS // N_KV_HEADS
WINDOW = 128
ROPE_THETA = 10000.0
RET_HEADS = 4
RET_QK_DIM = 128
RET_V_DIM = 2 * RET_QK_DIM
RET_CHUNK = 128
RET_THETA = 10000.0
D_FF = 4 * D_MODEL
EPS = 1e-6

ATT_Q = N_Q_HEADS * HEAD_DIM
ATT_KV = N_KV_HEADS * HEAD_DIM
RET_QK = RET_HEADS * RET_QK_DIM
RET_V = RET_HEADS * RET_V_DIM
SPLIT_SIZES = (ATT_Q, ATT_KV, ATT_KV, RET_QK, RET_QK, RET_V, RET_V, D_MODEL, D_MODEL)
W_IN = sum(SPLIT_SIZES)
SPLIT_POINTS = tuple(int(v) for v in np.cumsum(SPLIT_SIZES)[:-1])


def rmsnorm(x, g):
    xf = x.astype(jnp.float32)
    y = xf * lax.rsqrt(jnp.mean(xf * xf, axis=-1, keepdims=True) + EPS)
    return (y * g.astype(jnp.float32)).astype(x.dtype)

def rope_half(x, pos):
    half = x.shape[-1] // 2
    inv = ROPE_THETA ** (-jnp.arange(half, dtype=jnp.float32) / half)
    ang = pos.astype(jnp.float32)[:, None] * inv[None, :]
    cos = jnp.cos(ang)[None, :, None, :]
    sin = jnp.sin(ang)[None, :, None, :]
    xf = x.astype(jnp.float32)
    x1, x2 = xf[..., :half], xf[..., half:]
    return jnp.concatenate([x1 * cos - x2 * sin, x2 * cos + x1 * sin], axis=-1).astype(x.dtype)

def rotate_every_two(x):
    x1, x2 = x[..., ::2], x[..., 1::2]
    return jnp.stack([-x2, x1], axis=-1).reshape(x.shape)

def retention_rotation(x, pos):
    dk = x.shape[-1]
    theta = 1.0 / (RET_THETA ** jnp.linspace(0.0, 1.0, dk // 2, dtype=jnp.float32))
    theta = jnp.repeat(theta, 2)
    ang = pos.astype(jnp.float32)[:, None] * theta[None, :]
    cos = jnp.cos(ang)[None, :, None, :]
    sin = jnp.sin(ang)[None, :, None, :]
    xf = x.astype(jnp.float32)
    return (xf * cos + rotate_every_two(xf) * sin).astype(x.dtype)

def sliding_window_sink_attention(q, k, v, sinks):
    B, S = q.shape[0], q.shape[1]
    C = WINDOW
    nb = S // C
    qb = q.reshape(B, nb, C, N_KV_HEADS, GQA_GROUP, HEAD_DIM)
    kb = k.reshape(B, nb, C, N_KV_HEADS, HEAD_DIM)
    vb = v.reshape(B, nb, C, N_KV_HEADS, HEAD_DIM)

    def band(t):
        prev = jnp.pad(t, ((0, 0), (1, 0), (0, 0), (0, 0), (0, 0)))[:, :-1]
        return jnp.concatenate([prev, t], axis=2)

    kk, vv = band(kb), band(vb)
    s = jnp.einsum('bnqhgd,bnkhd->bnhgqk', qb, kk).astype(jnp.float32) * (HEAD_DIM ** -0.5)
    qi = jnp.arange(C)[:, None] + C
    kj = jnp.arange(2 * C)[None, :]
    rel = qi - kj
    valid = (rel >= 0) & (rel < WINDOW)
    first = (jnp.arange(nb) > 0)[:, None, None] | (kj >= C)[None]
    mask = valid[None] & first
    s = jnp.where(mask[None, :, None, None], s, -jnp.inf)
    sink = jnp.broadcast_to(
        sinks.astype(jnp.float32).reshape(1, 1, N_KV_HEADS, GQA_GROUP, 1, 1),
        s.shape[:-1] + (1,))
    p = jax.nn.softmax(jnp.concatenate([s, sink], axis=-1), axis=-1)[..., :-1]
    o = jnp.einsum('bnhgqk,bnkhd->bnqhgd', p.astype(v.dtype), vv)
    return o.reshape(B, S, ATT_Q)

def chunkwise_retention(q, k, v):
    B, S = q.shape[0], q.shape[1]
    C = RET_CHUNK
    nc = S // C
    log_g = jnp.log(1.0 - 2.0 ** (-5.0 - jnp.arange(RET_HEADS, dtype=jnp.float32)))
    idx = jnp.arange(C, dtype=jnp.float32)
    rel = idx[:, None] - idx[None, :]
    dmask = jnp.where(rel[None] >= 0, jnp.exp(log_g[:, None, None] * jnp.maximum(rel, 0.0)[None]), 0.0)

    qc = q.astype(jnp.float32).reshape(B, nc, C, RET_HEADS, RET_QK_DIM)
    kc = k.astype(jnp.float32).reshape(B, nc, C, RET_HEADS, RET_QK_DIM)
    vc = v.astype(jnp.float32).reshape(B, nc, C, RET_HEADS, RET_V_DIM)

    s = jnp.einsum('bnihd,bnjhd->bnhij', qc, kc) * dmask[None, None]
    inner = jnp.einsum('bnhij,bnjhe->bnihe', s, vc)

    zeta = jnp.exp(log_g[None, :] * (C - 1.0 - idx)[:, None])
    kv = jnp.einsum('bnjhd,bnjhe->nbhde', kc, vc * zeta[None, None, :, :, None])
    g_chunk = jnp.exp(log_g * C)[None, :, None, None]

    def step(R, kv_n):
        return R * g_chunk + kv_n, R

    R0 = jnp.zeros((B, RET_HEADS, RET_QK_DIM, RET_V_DIM), jnp.float32)
    _, R_prev = lax.scan(step, R0, kv)
    xi = jnp.exp(log_g[None, :] * (idx + 1.0)[:, None])
    cross = jnp.einsum('bnihd,nbhde->bnihe', qc, R_prev) * xi[None, None, :, :, None]
    return (inner + cross).reshape(B, S, RET_HEADS, RET_V_DIM)

def hybrid_layer(x, g_mix, w_in, sinks, w_a, w_b, w_out, g_mlp, w_up, w_down):
    B, S, _ = x.shape
    pos = jnp.arange(S)
    h = rmsnorm(x, g_mix)
    z = h @ w_in
    aq, ak, av, rq, rk, rv, rg, ga, gb = jnp.split(z, SPLIT_POINTS, axis=-1)

    aq = rope_half(aq.reshape(B, S, N_Q_HEADS, HEAD_DIM), pos)
    ak = rope_half(ak.reshape(B, S, N_KV_HEADS, HEAD_DIM), pos)
    av = av.reshape(B, S, N_KV_HEADS, HEAD_DIM)
    ya = sliding_window_sink_attention(aq, ak, av, sinks) @ w_a

    rq = retention_rotation(rq.reshape(B, S, RET_HEADS, RET_QK_DIM), pos)
    rk = retention_rotation(rk.reshape(B, S, RET_HEADS, RET_QK_DIM), pos) * (RET_QK_DIM ** -0.5)
    rv = rv.reshape(B, S, RET_HEADS, RET_V_DIM)
    r = chunkwise_retention(rq, rk, rv)
    r = r * lax.rsqrt(jnp.mean(r * r, axis=-1, keepdims=True) + EPS)
    r = r.reshape(B, S, RET_V) * jax.nn.silu(rg.astype(jnp.float32))
    yb = r.astype(x.dtype) @ w_b

    mixed = jax.nn.sigmoid(ga) * ya + jax.nn.sigmoid(gb) * yb
    x = x + mixed @ w_out

    h2 = rmsnorm(x, g_mlp)
    x = x + jnp.square(jax.nn.relu(h2 @ w_up)) @ w_down
    return x

def first_inputs(seed: int = 0) -> dict:
    key = jax.random.key(seed)
    ks = jax.random.split(key, 12)
    f32 = jnp.float32

    def nrm(k, shape, fan_in):
        return jax.random.normal(k, shape, f32) * (fan_in ** -0.5)

    return {
        "x": jax.random.normal(ks[0], (BATCH, SEQ, D_MODEL), f32),
        "g_mix": 1.0 + 0.05 * jax.random.normal(ks[1], (DEPTH, D_MODEL), f32),
        "w_in": nrm(ks[2], (DEPTH, D_MODEL, W_IN), D_MODEL),
        "sinks": 0.5 * jax.random.normal(ks[3], (DEPTH, N_Q_HEADS), f32),
        "w_a": nrm(ks[4], (DEPTH, ATT_Q, D_MODEL), ATT_Q),
        "w_b": nrm(ks[5], (DEPTH, RET_V, D_MODEL), RET_V),
        "w_out": nrm(ks[6], (DEPTH, D_MODEL, D_MODEL), D_MODEL),
        "g_mlp": 1.0 + 0.05 * jax.random.normal(ks[7], (DEPTH, D_MODEL), f32),
        "w_up": nrm(ks[8], (DEPTH, D_MODEL, D_FF), D_MODEL),
        "w_down": nrm(ks[9], (DEPTH, D_FF, D_MODEL), D_FF),
        "g_final": 1.0 + 0.05 * jax.random.normal(ks[10], (D_MODEL,), f32),
    }

def first_block(x, g_mix, w_in, sinks, w_a, w_b, w_out, g_mlp, w_up, w_down, g_final):
    for l in range(DEPTH):
        x = hybrid_layer(x, g_mix[l], w_in[l], sinks[l], w_a[l], w_b[l], w_out[l],
                         g_mlp[l], w_up[l], w_down[l])
    return rmsnorm(x, g_final)


ATT_WIDTH = D_MODEL // 2
HEAD_DIM_2 = 128
ATT_HEADS = ATT_WIDTH // HEAD_DIM_2
ROT_DIM = HEAD_DIM_2 // 4
ROPE_THETA_2 = 500000.0
MOBA_BLOCK = 256
MOBA_TOPK = 3
Q_CHUNK = 128
POOL_WIDTH = D_MODEL // 2
POOL_WINDOWS = (2, 4, 8, 16)
POOL_GROUPS = len(POOL_WINDOWS)
POOL_GROUP_W = POOL_WIDTH // POOL_GROUPS
EVEN_IN = 4 * ATT_WIDTH + 2 * POOL_WIDTH

S5_WIDTH = D_MODEL // 2
S5_GROUP_IN = 16
S5_GROUPS = S5_WIDTH // S5_GROUP_IN
S5_STATE = 64
CONV_WIDTH = D_MODEL // 2
CONV_K = 31
ODD_IN = 2 * S5_WIDTH + 3 * CONV_WIDTH

N_EVEN = (DEPTH + 1) // 2
N_ODD = DEPTH // 2
NEG = -1e30


def rms_norm(x, g):
    xf = x.astype(jnp.float32)
    y = xf * lax.rsqrt(jnp.mean(xf * xf, axis=-1, keepdims=True) + EPS) * g.astype(jnp.float32)
    return y.astype(x.dtype)

def rope_partial(x):
    s = x.shape[1]
    pos = jnp.arange(s, dtype=jnp.float32)
    inv = jnp.power(ROPE_THETA_2, -jnp.arange(0, ROT_DIM, 2, dtype=jnp.float32) / ROT_DIM)
    ang = pos[:, None] * inv[None, :]
    cos = jnp.cos(ang)[None, :, None, :]
    sin = jnp.sin(ang)[None, :, None, :]
    xf = x.astype(jnp.float32)
    x1 = xf[..., : ROT_DIM // 2]
    x2 = xf[..., ROT_DIM // 2: ROT_DIM]
    out = jnp.concatenate([x1 * cos - x2 * sin, x2 * cos + x1 * sin, xf[..., ROT_DIM:]], axis=-1)
    return out.astype(x.dtype)

def moba_attention(q, k, v):
    b, s, h, hd = q.shape
    nb = -(-s // MOBA_BLOCK)
    pad = nb * MOBA_BLOCK - s
    kp = jnp.pad(k, ((0, 0), (0, pad), (0, 0), (0, 0)))
    vp = jnp.pad(v, ((0, 0), (0, pad), (0, 0), (0, 0)))
    kb = kp.reshape(b, nb, MOBA_BLOCK, h, hd)
    vb = vp.reshape(b, nb, MOBA_BLOCK, h, hd)
    kbar = jnp.mean(kb.astype(jnp.float32), axis=2)
    gate = jnp.einsum('bshd,bnhd->bshn', q.astype(jnp.float32), kbar)
    qblk = jnp.arange(s) // MOBA_BLOCK
    past = jnp.arange(nb)[None, :] < qblk[:, None]
    gate = jnp.where(past[None, :, None, :], gate, -jnp.inf)
    n_sel = min(MOBA_TOPK, nb)
    _, idx = lax.top_k(gate, n_sel)
    valid = idx < qblk[None, :, None, None]

    nc = s // Q_CHUNK
    q_c = q.reshape(b, nc, Q_CHUNK, h, hd)
    idx_c = idx.reshape(b, nc, Q_CHUNK, h, n_sel)
    valid_c = valid.reshape(b, nc, Q_CHUNK, h, n_sel)
    kh = kb.transpose(0, 3, 1, 2, 4)
    vh = vb.transpose(0, 3, 1, 2, 4)
    scale = 1.0 / math.sqrt(hd)
    h_ar = jnp.arange(h)[None, :, None]

    def per_batch(args):
        qb, ib, mb, khb, vhb = args

        def per_chunk(cargs):
            c, qc, ic, mc = cargs
            kg = khb[h_ar, ic]
            vg = vhb[h_ar, ic]
            blk = (c * Q_CHUNK) // MOBA_BLOCK
            ko = lax.dynamic_index_in_dim(khb, blk, axis=1, keepdims=False)
            vo = lax.dynamic_index_in_dim(vhb, blk, axis=1, keepdims=False)
            s_sel = jnp.einsum('qhd,qhjkd->qhjk', qc, kg).astype(jnp.float32) * scale
            s_sel = jnp.where(mc[..., None], s_sel, NEG)
            s_own = jnp.einsum('qhd,hkd->qhk', qc, ko).astype(jnp.float32) * scale
            qpos = c * Q_CHUNK + jnp.arange(Q_CHUNK)
            kpos = blk * MOBA_BLOCK + jnp.arange(MOBA_BLOCK)
            causal = (kpos[None, :] <= qpos[:, None])[:, None, :]
            s_own = jnp.where(causal, s_own, NEG)
            sc = jnp.concatenate([s_sel.reshape(Q_CHUNK, h, n_sel * MOBA_BLOCK), s_own], axis=-1)
            p = jax.nn.softmax(sc, axis=-1).astype(vhb.dtype)
            p_sel = p[..., : n_sel * MOBA_BLOCK].reshape(Q_CHUNK, h, n_sel, MOBA_BLOCK)
            p_own = p[..., n_sel * MOBA_BLOCK:]
            return (jnp.einsum('qhjk,qhjkd->qhd', p_sel, vg)
                    + jnp.einsum('qhk,hkd->qhd', p_own, vo))

        return lax.map(per_chunk, (jnp.arange(nc), qb, ib, mb))

    out = lax.map(per_batch, (q_c, idx_c, valid_c, kh, vh))
    return out.reshape(b, s, h, hd)

def multiscale_pool(u, pool_w, pool_scale):
    b, s, _ = u.shape
    ug = u.reshape(b, s, POOL_GROUPS, POOL_GROUP_W).astype(jnp.float32)
    cs = jnp.concatenate([jnp.zeros((b, 1, POOL_GROUPS, POOL_GROUP_W), jnp.float32),
                          jnp.cumsum(ug, axis=1)], axis=1)
    t = jnp.arange(s)
    outs = []
    for g, w in enumerate(POOL_WINDOWS):
        lo = jnp.maximum(t + 1 - w, 0)
        win = cs[:, 1:, g] - cs[:, lo, g]
        cnt = (t + 1 - lo).astype(jnp.float32)[None, :, None]
        outs.append(win / cnt - ug[:, :, g])
    m = jnp.stack(outs, axis=2)
    y = jnp.einsum('bsgc,gcd->bsgd', m, pool_w.astype(jnp.float32)).reshape(b, s, POOL_WIDTH)
    return (y * pool_scale.astype(jnp.float32)).astype(u.dtype)

def s5_ssm(u, lam_re, lam_im, log_dt, b_re, b_im, c_re, c_im, d):
    bsz, s, _ = u.shape
    f32 = jnp.float32
    uf = u.reshape(bsz, s, S5_GROUPS, S5_GROUP_IN).astype(f32)
    lr, li = lam_re.astype(f32), lam_im.astype(f32)
    dt = jnp.exp(log_dt.astype(f32))[:, None]
    mag = jnp.exp(lr * dt)
    ab_re = mag * jnp.cos(li * dt)
    ab_im = mag * jnp.sin(li * dt)
    den = lr * lr + li * li
    num_re = ab_re - 1.0
    f_re = (num_re * lr + ab_im * li) / den
    f_im = (ab_im * lr - num_re * li) / den
    br, bi = b_re.astype(f32), b_im.astype(f32)
    bb_re = f_re[..., None] * br - f_im[..., None] * bi
    bb_im = f_re[..., None] * bi + f_im[..., None] * br
    bu_re = jnp.einsum('bsgi,gpi->bsgp', uf, bb_re)
    bu_im = jnp.einsum('bsgi,gpi->bsgp', uf, bb_im)
    a_re = jnp.broadcast_to(ab_re, bu_re.shape)
    a_im = jnp.broadcast_to(ab_im, bu_im.shape)

    def combine(e1, e2):
        a1r, a1i, b1r, b1i = e1
        a2r, a2i, b2r, b2i = e2
        return (a2r * a1r - a2i * a1i,
                a2r * a1i + a2i * a1r,
                a2r * b1r - a2i * b1i + b2r,
                a2r * b1i + a2i * b1r + b2i)

    _, _, xr, xi = lax.associative_scan(combine, (a_re, a_im, bu_re, bu_im), axis=1)
    y = (jnp.einsum('bsgp,gip->bsgi', xr, c_re.astype(f32))
         - jnp.einsum('bsgp,gip->bsgi', xi, c_im.astype(f32)))
    y = y.reshape(bsz, s, S5_WIDTH) + d.astype(f32) * u.astype(f32)
    return y.astype(u.dtype)

def conformer_conv(a, gl, dw, ln_g, ln_b, pw):
    g = a * jax.nn.sigmoid(gl)
    kern = dw.reshape(CONV_K, 1, CONV_WIDTH).astype(g.dtype)
    c = lax.conv_general_dilated(g, kern, window_strides=(1,), padding=[(CONV_K - 1, 0)],
                                 dimension_numbers=('NWC', 'WIO', 'NWC'),
                                 feature_group_count=CONV_WIDTH)
    cf = c.astype(jnp.float32)
    mu = jnp.mean(cf, axis=-1, keepdims=True)
    var = jnp.mean(jnp.square(cf - mu), axis=-1, keepdims=True)
    n = (cf - mu) * lax.rsqrt(var + EPS) * ln_g.astype(jnp.float32) + ln_b.astype(jnp.float32)
    return (jax.nn.silu(n).astype(a.dtype)) @ pw

def even_mixer(h, w_in, pool_w, pool_scale, w_out):
    b, s, _ = h.shape
    z = h @ w_in
    A = ATT_WIDTH
    q, k, v, ga, pu, gb = jnp.split(z, [A, 2 * A, 3 * A, 4 * A, 4 * A + POOL_WIDTH], axis=-1)
    q = rope_partial(q.reshape(b, s, ATT_HEADS, HEAD_DIM_2))
    k = rope_partial(k.reshape(b, s, ATT_HEADS, HEAD_DIM_2))
    v = v.reshape(b, s, ATT_HEADS, HEAD_DIM_2)
    att = moba_attention(q, k, v).reshape(b, s, A) * jax.nn.silu(ga)
    pool = multiscale_pool(pu, pool_w, pool_scale) * jax.nn.silu(gb)
    return jnp.concatenate([att, pool], axis=-1) @ w_out

def odd_mixer(h, w_in, lam_re, lam_im, log_dt, b_re, b_im, c_re, c_im, d,
              glu_w, glu_b, dw, ln_g, ln_b, pw, w_out):
    z = h @ w_in
    Wc, Wd = S5_WIDTH, CONV_WIDTH
    su, gc, ca, cb, gd = jnp.split(z, [Wc, 2 * Wc, 2 * Wc + Wd, 2 * Wc + 2 * Wd], axis=-1)
    y = s5_ssm(su, lam_re, lam_im, log_dt, b_re, b_im, c_re, c_im, d)
    ya, yb = jnp.split(y @ glu_w + glu_b, 2, axis=-1)
    ssm_out = ya * jax.nn.sigmoid(yb) * jax.nn.silu(gc)
    conv_out = conformer_conv(ca, cb, dw, ln_g, ln_b, pw) * jax.nn.silu(gd)
    return jnp.concatenate([ssm_out, conv_out], axis=-1) @ w_out

def second_inputs(seed: int = 0) -> dict:
    key = jax.random.key(seed)
    ks = jax.random.split(key, 24)
    nrm = jax.random.normal
    f32 = jnp.float32
    D = D_MODEL
    x = nrm(ks[0], (BATCH, SEQ, D), f32)
    pre_norm_g = 1.0 + 0.05 * nrm(ks[1], (DEPTH, D), f32)
    post_norm_g = 1.0 + 0.05 * nrm(ks[2], (DEPTH, D), f32)
    e_w_in = nrm(ks[3], (N_EVEN, D, EVEN_IN), f32) * D ** -0.5
    e_pool_w = nrm(ks[4], (N_EVEN, POOL_GROUPS, POOL_GROUP_W, POOL_GROUP_W), f32) * POOL_GROUP_W ** -0.5
    e_pool_scale = 1.0 + 0.05 * nrm(ks[5], (N_EVEN, POOL_WIDTH), f32)
    e_w_out = nrm(ks[6], (N_EVEN, ATT_WIDTH + POOL_WIDTH, D), f32) * (ATT_WIDTH + POOL_WIDTH) ** -0.5
    o_w_in = nrm(ks[7], (N_ODD, D, ODD_IN), f32) * D ** -0.5
    n_idx = jnp.arange(S5_STATE, dtype=f32)
    o_lam_re = -0.5 + 0.01 * nrm(ks[8], (N_ODD, S5_GROUPS, S5_STATE), f32)
    o_lam_im = math.pi * n_idx[None, None, :] + 0.01 * nrm(ks[9], (N_ODD, S5_GROUPS, S5_STATE), f32)
    o_log_dt = jax.random.uniform(ks[10], (N_ODD, S5_GROUPS), f32, math.log(1e-3), math.log(1e-1))
    o_b_re = nrm(ks[11], (N_ODD, S5_GROUPS, S5_STATE, S5_GROUP_IN), f32) * (2.0 * S5_GROUP_IN) ** -0.5
    o_b_im = nrm(ks[12], (N_ODD, S5_GROUPS, S5_STATE, S5_GROUP_IN), f32) * (2.0 * S5_GROUP_IN) ** -0.5
    o_c_re = nrm(ks[13], (N_ODD, S5_GROUPS, S5_GROUP_IN, S5_STATE), f32) * (2.0 * S5_STATE) ** -0.5
    o_c_im = nrm(ks[14], (N_ODD, S5_GROUPS, S5_GROUP_IN, S5_STATE), f32) * (2.0 * S5_STATE) ** -0.5
    o_d = nrm(ks[15], (N_ODD, S5_WIDTH), f32)
    o_glu_w = nrm(ks[16], (N_ODD, S5_WIDTH, 2 * S5_WIDTH), f32) * S5_WIDTH ** -0.5
    o_glu_b = 0.01 * nrm(ks[17], (N_ODD, 2 * S5_WIDTH), f32)
    o_dw = nrm(ks[18], (N_ODD, CONV_K, CONV_WIDTH), f32) * CONV_K ** -0.5
    o_ln_g = 1.0 + 0.05 * nrm(ks[19], (N_ODD, CONV_WIDTH), f32)
    o_ln_b = 0.01 * nrm(ks[20], (N_ODD, CONV_WIDTH), f32)
    o_pw = nrm(ks[21], (N_ODD, CONV_WIDTH, CONV_WIDTH), f32) * CONV_WIDTH ** -0.5
    o_w_out = nrm(ks[22], (N_ODD, S5_WIDTH + CONV_WIDTH, D), f32) * (S5_WIDTH + CONV_WIDTH) ** -0.5
    return {"x": x, "pre_norm_g": pre_norm_g, "post_norm_g": post_norm_g,
            "e_w_in": e_w_in, "e_pool_w": e_pool_w, "e_pool_scale": e_pool_scale, "e_w_out": e_w_out,
            "o_w_in": o_w_in, "o_lam_re": o_lam_re, "o_lam_im": o_lam_im, "o_log_dt": o_log_dt,
            "o_b_re": o_b_re, "o_b_im": o_b_im, "o_c_re": o_c_re, "o_c_im": o_c_im, "o_d": o_d,
            "o_glu_w": o_glu_w, "o_glu_b": o_glu_b, "o_dw": o_dw, "o_ln_g": o_ln_g, "o_ln_b": o_ln_b,
            "o_pw": o_pw, "o_w_out": o_w_out}

def second_block(x, pre_norm_g, post_norm_g, e_w_in, e_pool_w, e_pool_scale, e_w_out,
              o_w_in, o_lam_re, o_lam_im, o_log_dt, o_b_re, o_b_im, o_c_re, o_c_im, o_d,
              o_glu_w, o_glu_b, o_dw, o_ln_g, o_ln_b, o_pw, o_w_out):
    for i in range(DEPTH):
        h = rms_norm(x, pre_norm_g[i])
        j = i // 2
        if i % 2 == 0:
            y = even_mixer(h, e_w_in[j], e_pool_w[j], e_pool_scale[j], e_w_out[j])
        else:
            y = odd_mixer(h, o_w_in[j], o_lam_re[j], o_lam_im[j], o_log_dt[j], o_b_re[j], o_b_im[j],
                          o_c_re[j], o_c_im[j], o_d[j], o_glu_w[j], o_glu_b[j], o_dw[j],
                          o_ln_g[j], o_ln_b[j], o_pw[j], o_w_out[j])
        x = x + rms_norm(y, post_norm_g[i])
    return x


def setup_inputs(seed=0):
    out = dict(first_inputs(seed))
    for name, value in second_inputs(seed + 1).items():
        if name != "x":
            out[name + "_2"] = value
    return out


def reference(
    x, g_mix, w_in, sinks, w_a, w_b, w_out, g_mlp, w_up, w_down, g_final, pre_norm_g_2,
    post_norm_g_2, e_w_in_2, e_pool_w_2, e_pool_scale_2, e_w_out_2, o_w_in_2, o_lam_re_2,
    o_lam_im_2, o_log_dt_2, o_b_re_2, o_b_im_2, o_c_re_2, o_c_im_2, o_d_2, o_glu_w_2, o_glu_b_2,
    o_dw_2, o_ln_g_2, o_ln_b_2, o_pw_2, o_w_out_2,
):
    x = first_block(
        x, g_mix, w_in, sinks, w_a, w_b, w_out, g_mlp, w_up, w_down, g_final,
    )
    return second_block(
        x, pre_norm_g_2, post_norm_g_2, e_w_in_2, e_pool_w_2, e_pool_scale_2, e_w_out_2,
        o_w_in_2, o_lam_re_2, o_lam_im_2, o_log_dt_2, o_b_re_2, o_b_im_2, o_c_re_2, o_c_im_2,
        o_d_2, o_glu_w_2, o_glu_b_2, o_dw_2, o_ln_g_2, o_ln_b_2, o_pw_2, o_w_out_2,
    )


_drawn_inputs = setup_inputs


def setup_inputs(seed=0):
    import zlib

    import numpy as np

    out = dict(_drawn_inputs(seed))
    spreads = {}
    factors = {'o_lam_re_2': 8.0,
     'o_b_re_2': 2.979,
     'o_b_im_2': 3.315,
     'o_c_re_2': 2.919,
     'o_c_im_2': 3.127,
     'o_glu_b_2': 8.0,
     'o_ln_b_2': 8.0}
    for name, (base, spread) in spreads.items():
        noise = np.random.default_rng([zlib.crc32(name.encode()), seed]).standard_normal(out[name].shape)
        drawn = base * np.exp(spread * noise) if base else spread * noise
        out[name] = jnp.asarray(drawn.astype(out[name].dtype))
    for name, factor in factors.items():
        out[name] = (out[name] * factor).astype(out[name].dtype)
    return out
```

```python
from contextlib import ExitStack

import concourse.bass as bass
import numpy as np
from concourse import mybir

F32 = mybir.dt.float32
F32R = mybir.dt.float32r
ALU = mybir.AluOpType
ACT = mybir.ActivationFunctionType
AX_X = mybir.AxisListType.X

P = 128
D = 1024
SEQ = 256
DEPTH = 2
T = SEQ // P
KD = D // P
COLS = 512
KP = 4
EPS = 1e-6
FF = 4 * D
F_GROUPS = FF // COLS

HEAD = 64
Q_HEADS = 8
KV_HEADS = 2
PAIRS = Q_HEADS // 2
RET_HEADS = 4
RET_QK = 128
RET_V = 256
ATT2_HEADS = 4
ROT2 = 32
POOL_WINDOWS = (2, 4, 8, 16)
POOL_PAD = 16
S5_STATE = 64
S5_IN = 16
S5_TILES = 16
CONV_K = 31
PE_CONV = 2
CHUNK = 11
CHUNKS = -(-PE_CONV * CONV_K // CHUNK)
HALF = 4
TWO_PI = 6.2831850
TO_TURNS = float(np.float32(1.0 / (2.0 * np.pi)))
ROUND = 12582912.0
NEG = -1e30

RQ, RK, AQ, AKV, RV0, RV1, RG0, RG1, GA0, GA1, GB0, GB1 = range(12)
W_IN_START = (768, 1280, 0, 512, 1792, 2304, 2816, 3328, 3840, 4352, 4864, 5376)
W_IN_GROUPS = len(W_IN_START)
AKV_WIDTH = 256

PIECE_A = 2 * W_IN_GROUPS
PIECE_B = PIECE_A + 2
PIECE_O = PIECE_B + 4
PIECE_MLP = PIECE_O + 4
UP_PIECE = [PIECE_MLP] + [PIECE_MLP + 4 * f - 2 for f in range(1, F_GROUPS)]
DOWN_PIECE = [PIECE_MLP + 4 + 4 * f for f in range(F_GROUPS - 1)] + [PIECE_MLP + 4 * F_GROUPS - 2]
ARENA = 19968
PIECES = PIECE_MLP + 4 * F_GROUPS
USE_YA = W_IN_GROUPS
USE_YB = USE_YA + 2
USE_O = USE_YB + 2
USE_UP = USE_O + 2
USES = USE_UP + F_GROUPS
E_PIECE = DEPTH * PIECES
E_OUT_PIECE = E_PIECE + 12
O_PIECE = E_OUT_PIECE + 4
GLU_PIECE = O_PIECE + 10
PW_PIECE = GLU_PIECE + 2
O_OUT_PIECE = PW_PIECE + 1
ALL_PIECES = O_OUT_PIECE + 4
E_USE = DEPTH * USES
E_OUT_USE = E_USE + 6
O_USE = E_OUT_USE + 2
GLU_USE = O_USE + 5
PW_USE = GLU_USE + 2
O_OUT_USE = PW_USE + 1
SU, CA, CB, GC, GD = range(5)
O_START = (0, 1024, 1536, 512, 2048)

NORMS = 2 * DEPTH + 5

POOL_PIECES = (GLU_PIECE + 1, PW_PIECE, O_OUT_PIECE, O_OUT_PIECE + 1)
RAW_RING = 2
WARM, WARM_WAIT = 9, 8
SPLIT_RING = 3
AHEAD = 2

V_MIX, V_MLP, V_PRE, V_LRE, V_LIM, V_PSC, V_D, V_GLUB, V_LNG, V_LNB, V_ROWS = (
    0, 16, 32, 48, 64, 80, 84, 88, 96, 100, 104)


KEPT_TABLES = ("ident", "minus_half", "odd_group_row", "odd_group_state")


def shape_constants():
    f = np.float32
    part = np.arange(P)
    pos = np.arange(SEQ, dtype=f)
    tabs = {"ident": np.eye(P, dtype=f), "minus_half": np.full((P, 4), -0.5)}

    def by_tile(a):
        return np.concatenate([a[t * P:(t + 1) * P] for t in range(T)], axis=1)

    half = HEAD // 2
    ang = pos[:, None] * (f(10000.0) ** (-np.arange(half, dtype=f) / f(half)))[None]
    tabs["att_cos"], tabs["att_sin"] = by_tile(np.cos(ang)), by_tile(np.sin(ang))
    theta = (f(1.0) / (f(10000.0) ** np.linspace(0.0, 1.0, RET_QK // 2, dtype=f))).astype(f)
    ang = pos[:, None] * np.repeat(theta, 2)[None]
    tabs["ret_cos"], tabs["ret_sin"] = by_tile(np.cos(ang)), by_tile(np.sin(ang))
    log_g = np.log(1.0 - 2.0 ** (-5.0 - np.arange(RET_HEADS)))
    rel = part[None, :] - part[:, None]
    key_scale = RET_QK ** -0.5
    tabs["decay"] = np.concatenate(
        [np.where(rel >= 0, np.exp(g * np.maximum(rel, 0)), 0.0) for g in log_g], axis=1) * key_scale
    tabs["zeta"] = np.exp(log_g[None] * (P - 1.0 - part)[:, None]) * key_scale
    tabs["xi"] = np.broadcast_to(np.exp(log_g[:, None] * (part + 1.0)[None]).reshape(1, -1), (P, RET_HEADS * P))
    causal = np.where(part[None, :] <= part[:, None], 0.0, NEG)
    before = np.where(part[None, :] > part[:, None], 0.0, NEG)
    tabs["window"] = np.concatenate([causal, before, causal], axis=1)
    tabs["causal"] = np.concatenate([causal, np.zeros((P, P)), causal], axis=1)
    inv = f(500000.0) ** (-np.arange(0, ROT2, 2, dtype=f) / f(ROT2))
    ang = pos[:, None] * inv[None].astype(f)
    tabs["att2_cos"], tabs["att2_sin"] = by_tile(np.cos(ang)), by_tile(np.sin(ang))
    first = np.arange(POOL_PAD)
    tabs["pool_first"] = np.broadcast_to(
        np.concatenate([1.0 / np.minimum(first + 1, w) for w in POOL_WINDOWS])[None], (P, 4 * POOL_PAD))
    tabs["time"] = np.broadcast_to(pos[None], (P, SEQ))
    tabs["odd_group_row"] = np.stack([(part // S5_IN) % 2 == g for g in range(2)], axis=1)
    tabs["odd_group_state"] = np.stack([part // S5_STATE == g for g in range(2)], axis=1)
    at, where = 0, {}
    order = [n for n in KEPT_TABLES] + [n for n in tabs if n not in KEPT_TABLES]
    for name in order:
        where[name] = (at, at + tabs[name].shape[1])
        at += tabs[name].shape[1]
    return np.ascontiguousarray(np.concatenate([tabs[n] for n in order], axis=1), dtype=f), where


def build_program(nc, ins, consts, where, out):
    ctx = ExitStack()
    with ctx:
        def sb(name, shape, dt=F32):
            return ctx.enter_context(nc.sbuf_tensor(name, shape, dt))

        def sem(name):
            return ctx.enter_context(nc.semaphore(name))

        const = sb("const", [P, consts.shape[1]])

        def tab(name):
            a, b = where[name]
            return const[:, a:b]

        ident = tab("ident")
        FIRST_TABLES = where[KEPT_TABLES[-1]][1]
        conv_diag = const[:, FIRST_TABLES:FIRST_TABLES + 2 * CHUNK * P].rearrange("p (k c) -> p k c", c=P)
        raw = sb("raw", [P, RAW_RING, KP, COLS])
        w_hi = sb("w_hi", [P, SPLIT_RING, KP, COLS], F32R)
        w_lo = sb("w_lo", [P, SPLIT_RING, KP, COLS], F32R)
        x = sb("x_sb", [P, T, D])
        h = sb("h_sb", [P, T, D])
        hT_hi = sb("hT_hi", [P, KD, SEQ], F32R)
        hT_lo = sb("hT_lo", [P, KD, SEQ], F32R)
        uT_at = nc.sbuf_base
        uT_hi = sb("uT_hi", [P, KD, SEQ], F32R)
        uT_lo = sb("uT_lo", [P, KD, SEQ], F32R)
        uT_bytes = KD * SEQ * 4
        pool_w = nc.alloc_sbuf_tensor_at("pool_w", [P, HALF, P], F32, offset=uT_at)
        pool_m = nc.alloc_sbuf_tensor_at("pool_m", [P, HALF, SEQ], F32, offset=uT_at + uT_bytes)
        b_mat = nc.alloc_sbuf_tensor_at("b_mat", [P, 2, HALF, P], F32, offset=uT_at)
        s5_part = nc.alloc_sbuf_tensor_at("s5_part", [P, HALF, SEQ], F32, offset=uT_at + uT_bytes // 2)
        c_mat = nc.alloc_sbuf_tensor_at("c_mat", [P, 3, HALF, P], F32, offset=uT_at + uT_bytes)
        rows = sb("rows", [P, P])
        conv_rows = sb("conv_rows", [P, P])
        dt_rows = sb("dt_rows", [S5_TILES, 2, S5_STATE])
        log_dt = sb("log_dt", [S5_TILES, 2])
        vec = sb("vec", [P, V_ROWS])
        conv_w = sb("conv_w", [P, CONV_K, HALF])
        s5_dt = sb("s5_dt", [P, S5_TILES])
        sink = sb("sink", [P, DEPTH, Q_HEADS])
        ssq = sb("ssq", [P, NORMS, T, 2])
        mean = sb("mean", [P, NORMS, T])
        rstd = sb("rstd", [P, NORMS, T])
        half_rstd = sb("half_rstd", [P, DEPTH, T])
        rstd2 = sb("rstd2", [P, DEPTH, T])
        final_inv = sb("final_inv", [P, T])
        ret_ss = sb("ret_ss", [P, T, RET_HEADS])
        ret_ms = sb("ret_ms", [P, T, RET_HEADS])
        ret_rstd = sb("ret_rstd", [P, T, RET_HEADS])
        top = sb("top", [P, 2, T])
        neg_top = sb("neg_top", [P, 2, T])
        sink_gap = sb("sink_gap", [P, 2, T])
        sink_exp = sb("sink_exp", [P, 2, T])
        den = sb("den", [P, 2, T])
        den_all = sb("den_all", [P, 2, T])
        inv_den = sb("inv_den", [P, 2, T])
        top2 = sb("top2", [P, ATT2_HEADS, T])
        neg_top2 = sb("neg_top2", [P, ATT2_HEADS, T])
        den2 = sb("den2", [P, ATT2_HEADS, T])
        inv_den2 = sb("inv_den2", [P, ATT2_HEADS, T])
        s5_small = sb("s5_small", [P, 16, S5_TILES])
        ln_stat = sb("ln_stat", [P, T, 6])
        ln_mv = sb("ln_mv", [P, T, 2])
        ln_var = sb("ln_var", [P, T])
        ln_rstd = sb("ln_rstd", [P, T])

        arena = sb("arena", [P, ARENA])

        def area(start, *shape):
            n = int(np.prod(shape))
            assert start + n <= ARENA, (start, shape)
            v = arena[:, start:start + n]
            if len(shape) == 2:
                return v.rearrange("p (a b) -> p a b", a=shape[0])
            if len(shape) == 3:
                return v.rearrange("p (a b c) -> p a b c", a=shape[0], b=shape[1])
            return v

        z_ret = area(0, T, 2 * RET_HEADS * RET_QK)
        z_att = area(2048, T, 768)
        z_rv = area(3584, T, D)
        z_rg = area(5632, T, D)
        z_ga = area(7680, T, D)
        z_gb = area(9728, T, D)
        aqT = area(11776, PAIRS, SEQ)
        akT = area(12800, KV_HEADS, SEQ)
        rqT = area(13312, RET_HEADS, SEQ)
        rkT = area(14336, RET_HEADS, SEQ)
        rqT_xi = area(15360, RET_HEADS, P)
        s_ret = area(15872, T, RET_HEADS * P)
        kv_state = area(16896, RET_HEADS, RET_V)
        ak_twice = area(16896, T, KV_HEADS * 2 * HEAD)
        rk_zeta = area(17920, RET_HEADS * RET_QK)
        probs = area(18432, 2, 384)
        probsT = area(19200, 2, 384)
        rg_tanh = z_ga[:, :, 0:512]
        relu_buf = area(16384, 2, 512)
        sq_buf = area(17408, 2, 512)

        s5_cos = area(0, S5_TILES, SEQ)
        s5_sin = area(4096, S5_TILES, SEQ)
        s5_tmp = area(8192, S5_TILES, SEQ)
        g_final = area(12288, D)
        PW = POOL_PAD + SEQ
        xg = area(8192, T, D)
        final_junk = area(16384, 2 * T, 512)
        zq = area(8192, T, 512)
        zk = area(9216, T, 512)
        zv = area(10240, T, 512)
        q2T = area(11264, ATT2_HEADS, SEQ)
        k2T = area(12288, ATT2_HEADS, SEQ)
        probs2 = area(13312, ATT2_HEADS, 384)
        probs2T = area(11264, ATT2_HEADS, 384)
        mix_tmp = area(12288, KD, SEQ)
        sq_junk = area(12288, 2 * T, 512)
        b_in = area(14848, 2, S5_TILES, S5_IN)
        c_in = area(15360, 2, HALF, S5_STATE)
        pool_in = area(16384, HALF, PW)
        gate_a = area(17472, HALF, SEQ)
        gate_b = area(18496, HALF, SEQ)
        rot2_tmp = area(19520, 4, ATT2_HEADS * ROT2 // 2)
        pool_s1 = area(8192, HALF, PW)
        pool_s2 = area(8192 + HALF * PW, HALF - 1, PW)
        b_bar = area(16384, 4, S5_TILES, S5_IN)
        b_pad = area(8192, 2, S5_TILES, 2 * S5_IN)
        c_pad = area(9216, 2, HALF, P)
        g_post = [area(10240, D), area(0, D)]
        conv_out = area(8192, HALF, SEQ)
        conv_tok = area(9216, T, 512)
        su = area(10240, HALF, SEQ)
        s5_x = [[area(11264 + 2048 * b + 1024 * i, HALF, SEQ) for i in range(2)] for b in range(2)]
        s5_o = [h[:, i, :].rearrange("p (q t) -> p q t", q=HALF) for i in range(2)]
        y_ssm = area(15360, HALF, SEQ)
        gate_c = area(16384, HALF, SEQ)
        gate_d = area(17408, HALF, SEQ)
        CW = CONV_K - 1 + SEQ
        conv_in = area(18432, HALF, CW)
        conv_act = area(8192, HALF, SEQ)
        glu_a = area(11264, HALF, SEQ)
        glu_s = area(12288, HALF, SEQ)
        cat_tmp = area(13312, KD, SEQ)
        bank = ctx.enter_context(nc.psum_tensor("bank", [P, 8, 512], F32))
        OUT = [bank[:, 0, :], bank[:, 1, :]]
        PW_BANKS = [bank[:, 4 + b, :] for b in range(2)]
        TURN = [bank[:, i, :] for i in (3, 4, 6, 7)]
        ROWS_T = [bank[:, i, :] for i in (6, 7, 3, 4)]
        ACC = [[bank[:, 2, :], bank[:, 3, :]], [bank[:, 4, :], bank[:, 5, :]]]

        ident_landed = sem("ident_landed")
        const_landed = sem("const_landed")
        mix_landed = sem("mix_landed")
        rows_landed = sem("rows_landed")
        ldt_landed = sem("ldt_landed")
        sink_landed = sem("sink_landed")
        gfinal_landed = sem("gfinal_landed")
        poolw_landed = sem("poolw_landed")
        gpost_landed = [sem(f"gpost_landed{i}") for i in range(DEPTH)]
        s5_landed = sem("s5_landed")
        x_landed = [sem(f"x_landed{t}") for t in range(T)]
        raw_landed = [sem(f"raw_landed{i}") for i in range(RAW_RING)]
        hi_ready = sem("hi_ready")
        lo_ready = sem("lo_ready")
        lo_pool_ready = sem("lo_pool_ready")
        piece_used = sem("piece_used")
        out0_done = sem("out0_done")
        out_free = [sem(f"out_free{i}") for i in range(2)]
        dt_spread = sem("dt_spread")
        vec_turned = sem("vec_turned")
        vec_ready = sem("vec_ready")
        sq_done = [sem(f"sq_done{t}") for t in range(T)]
        mean_ready = sem("mean_ready")
        rstd_ready = sem("rstd_ready")
        half_ready = sem("half_ready")
        h_ready = sem("h_ready")
        warm_zero = sem("warm_zero")
        first_hi = sem("first_hi")
        first_lo = sem("first_lo")
        turned = sem("turned")
        turned_hi = sem("turned_hi")
        turned_lo = sem("turned_lo")
        rot_done = [sem(f"rot_done{t}") for t in range(T)]
        rope_done = [sem(f"rope_done{t}") for t in range(T)]
        ret_turned = sem("ret_turned")
        rqT_ready = sem("rqT_ready")
        rkT_ready = sem("rkT_ready")
        rqxi_ready = sem("rqxi_ready")
        rkz_ready = sem("rkz_ready")
        att_turned = sem("att_turned")
        aqT_first = sem("aqT_first")
        aqT_second = sem("aqT_second")
        akT_ready = sem("akT_ready")
        tanh_ready = sem("tanh_ready")
        s_ret_done = sem("s_ret_done")
        s_ret_ready = sem("s_ret_ready")
        scores_done = sem("scores_done")
        scores_read = sem("scores_read")
        top_ready = sem("top_ready")
        exp_done = sem("exp_done")
        probs_ready = sem("probs_ready")
        probs_turned = sem("probs_turned")
        probsT_even = sem("probsT_even")
        probsT_odd = sem("probsT_odd")
        pv_done = sem("pv_done")
        oT_hi = sem("oT_hi")
        oT_lo = sem("oT_lo")
        kv_done = sem("kv_done")
        kv_ready = sem("kv_ready")
        ret_done = sem("ret_done")
        ret_sq = sem("ret_sq")
        ret_mean = sem("ret_mean")
        ret_scale = sem("ret_scale")
        r_ready = sem("r_ready")
        m_ready = sem("m_ready")
        relu_done = sem("relu_done")
        up_hi = sem("up_hi")
        up_lo = sem("up_lo")
        x_mlp = sem("x_mlp")
        xg_ready = sem("xg_ready")
        final_scaled = sem("final_scaled")
        s5_decay_in = sem("s5_decay_in")
        s5_decay = sem("s5_decay")
        s5_angles = sem("s5_angles")
        s5_tables = sem("s5_tables")
        s5_den = sem("s5_den")
        s5_inv = sem("s5_inv")
        s5_padded = sem("s5_padded")
        s5_turned = sem("s5_turned")
        s5_mats = sem("s5_mats")
        rope2_done = sem("rope2_done")
        qk2_turned = sem("qk2_turned")
        q2T_ready = sem("q2T_ready")
        k2T_ready = sem("k2T_ready")
        scores2_done = sem("scores2_done")
        scores2_read = sem("scores2_read")
        top2_ready = sem("top2_ready")
        exp2_done = sem("exp2_done")
        probs2_ready = sem("probs2_ready")
        probs2_turned = sem("probs2_turned")
        probs2T_act = sem("probs2T_act")
        probs2T_dve = sem("probs2T_dve")
        pool_zero = sem("pool_zero")
        pool_mean = sem("pool_mean")
        pool_done = sem("pool_done")
        pv2_done = sem("pv2_done")
        cat_tmp_ready = sem("cat_tmp_ready")
        cat_hi = sem("cat_hi")
        cat_lo = sem("cat_lo")
        y_lo = sem("y_lo")
        post_ready = sem("post_ready")
        conv_zero = sem("conv_zero")
        conv_gated = sem("conv_gated")
        conv_diag_ready = sem("conv_diag_ready")
        conv_used = sem("conv_used")
        conv_taken = sem("conv_taken")
        conv_done = sem("conv_done")
        conv_turned = sem("conv_turned")
        ln_var_ready = sem("ln_var_ready")
        ln_scale = sem("ln_scale")
        ln_done = sem("ln_done")
        ln_turned = sem("ln_turned")
        conv_silu = sem("conv_silu")
        drive_done = sem("drive_done")
        drive_read = sem("drive_read")
        scans_done = sem("scans_done")
        states_ready = sem("states_ready")
        y_done = sem("y_done")
        y_ready = sem("y_ready")
        glu_ready = sem("glu_ready")
        x_final = sem("x_final")
        stored = sem("stored")
        act_order = sem("act_order")
        dve_order = sem("dve_order")
        pool_order = sem("pool_order")

        class Order:

            def __init__(self, eng, s):
                self.eng, self.sem, self.n = eng, s, 0

            def mark(self, ins):
                self.n += 1
                ins.then_inc(self.sem, 1)

            def settle(self):
                self.eng.wait_ge(self.sem, self.n)

            def link(self, ins):
                self.mark(ins)
                self.settle()

        def w_in_piece(l, g, half):
            n = AKV_WIDTH if g == AKV else COLS
            w = ins["w_in"][l].rearrange("(k p) n -> p k n", p=P)
            return w[:, half * KP:half * KP + KP, W_IN_START[g]:W_IN_START[g] + n]

        def square_piece(w, c, half):
            return w.rearrange("(k p) n -> p k n", p=P)[:, half * KP:half * KP + KP, c * COLS:(c + 1) * COLS]

        def last_piece(n):
            l, u = divmod(n, USES)
            if l < DEPTH:
                if u < USE_YA:
                    return l * PIECES + 2 * u + 1
                if u < USE_YB:
                    return l * PIECES + PIECE_A + u - USE_YA
                if u < USE_UP:
                    return l * PIECES + PIECE_B + 2 * (u - USE_YB) + 1
                return l * PIECES + UP_PIECE[u - USE_UP] + 1
            if n < GLU_USE:
                return E_PIECE + 2 * (n - E_USE) + 1
            if n < O_OUT_USE:
                return GLU_PIECE + n - GLU_USE
            return O_OUT_PIECE + 2 * (n - O_OUT_USE) + 1

        def stat_count(n, t):
            return T * (n if n <= 2 * DEPTH else n - 1) + t + 1

        def piece_split(eng, p):
            if p in POOL_PIECES:
                eng.wait_ge(lo_pool_ready, POOL_PIECES.index(p) + 1)
            else:
                eng.wait_ge(lo_ready, p + 1 - sum(i < p for i in POOL_PIECES))

        def whole(eng, n, t):
            if t == 0:
                eng.wait_ge(out0_done, n + 1)
            else:
                eng.wait_ge(piece_used, last_piece(n) + 1)

        def rotate_pairs(eng, o, l, t, tmp):
            for g in (RQ, RK):
                eng.wait_ge(out_free[t], l * USES + g + 1)
            heads = 2 * RET_HEADS
            z = z_ret[:, t, :]
            zp = z.rearrange("p (n d e) -> p n d e", n=heads, e=2)
            cos = tab("ret_cos")[:, t * RET_QK:(t + 1) * RET_QK].unsqueeze(1).broadcast_to([P, heads, RET_QK])
            sin = tab("ret_sin")[:, t * RET_QK:(t + 1) * RET_QK].rearrange("p (d e) -> p d e", e=2)[:, :, 0]
            sin = sin.unsqueeze(1).broadcast_to([P, heads, RET_QK // 2])
            a, b = tmp[:, 0, :], tmp[:, 1, :]
            bp = b.rearrange("p (n d e) -> p n d e", n=heads, e=2)
            o.mark(eng.tensor_tensor(a.rearrange("p (n d) -> p n d", n=heads), z.rearrange("p (n d) -> p n d", n=heads), cos, ALU.mult))
            ap = a.rearrange("p (n d e) -> p n d e", n=heads, e=2)
            o.mark(eng.tensor_tensor(bp[:, :, :, 0], zp[:, :, :, 1], sin, ALU.mult))
            o.mark(eng.tensor_tensor(bp[:, :, :, 1], zp[:, :, :, 0], sin, ALU.mult))
            o.settle()
            o.mark(eng.tensor_tensor(zp[:, :, :, 0], ap[:, :, :, 0], bp[:, :, :, 0], ALU.subtract))
            eng.tensor_tensor(zp[:, :, :, 1], ap[:, :, :, 1], bp[:, :, :, 1], ALU.add).then_inc(rot_done[t], 1)
            eng.wait_ge(rot_done[t], l + 1)

        def rotate_halves(eng, o, l, t, tmp):
            for g in (AQ, AKV):
                eng.wait_ge(out_free[t], l * USES + g + 1)
            heads = Q_HEADS + KV_HEADS
            half = HEAD // 2
            z = z_att[:, t, 0:heads * HEAD].rearrange("p (n e d) -> p n e d", n=heads, e=2)
            cos = tab("att_cos")[:, t * half:(t + 1) * half].unsqueeze(1).broadcast_to([P, 2 * heads, half])
            sin = tab("att_sin")[:, t * half:(t + 1) * half].unsqueeze(1).broadcast_to([P, heads, half])
            a, b = tmp[:, 0, 0:heads * HEAD], tmp[:, 1, 0:heads * HEAD]
            b4 = b.rearrange("p (n e d) -> p n e d", n=heads, e=2)
            o.mark(eng.tensor_tensor(a.rearrange("p (n d) -> p n d", d=half),
                                     z_att[:, t, 0:heads * HEAD].rearrange("p (n d) -> p n d", d=half), cos, ALU.mult))
            a4 = a.rearrange("p (n e d) -> p n e d", n=heads, e=2)
            o.mark(eng.tensor_tensor(b4[:, :, 0, :], z[:, :, 1, :], sin, ALU.mult))
            o.mark(eng.tensor_tensor(b4[:, :, 1, :], z[:, :, 0, :], sin, ALU.mult))
            o.settle()
            twice = ak_twice[:, t, :].rearrange("p (v c e d) -> p v c e d", v=KV_HEADS, c=2, e=2)
            for e, op in ((0, ALU.subtract), (1, ALU.add)):
                o.mark(eng.tensor_tensor(z[:, 0:Q_HEADS, e, :], a4[:, 0:Q_HEADS, e, :], b4[:, 0:Q_HEADS, e, :], op))
                for c in range(2):
                    last = eng.tensor_tensor(twice[:, :, c, e, :], a4[:, Q_HEADS:, e, :], b4[:, Q_HEADS:, e, :], op)
                    if e == 0 or c == 0:
                        o.mark(last)
            last.then_inc(rope_done[t], 1)
            eng.wait_ge(rope_done[t], l + 1)

        block = ctx.enter_context(nc.Block())

        @block.sync
        def _(sp):
            for t in range(T):
                sp.dma_start(x[:, t, :], ins["x"][0, t * P:(t + 1) * P, :]).then_inc(x_landed[t], 16)
            n = [0]

            def small_inputs():
                def vector_rows(at, v):
                    v = v.rearrange("(r c) -> r c", c=P)
                    sp.dma_start(rows[at:at + v.shape[0], :], v).then_inc(rows_landed, 16)

                vector_rows(V_MLP, ins["g_mlp"].rearrange("l d -> (l d)"))
                vector_rows(V_PRE, ins["pre_norm_g_2"].rearrange("l d -> (l d)"))
                vector_rows(V_LRE, ins["o_lam_re_2"].rearrange("a g p -> (a g p)"))
                vector_rows(V_LIM, ins["o_lam_im_2"].rearrange("a g p -> (a g p)"))
                vector_rows(V_PSC, ins["e_pool_scale_2"].rearrange("a d -> (a d)"))
                vector_rows(V_D, ins["o_d_2"].rearrange("a d -> (a d)"))
                vector_rows(V_GLUB, ins["o_glu_b_2"].rearrange("a d -> (a d)"))
                vector_rows(V_LNG, ins["o_ln_g_2"].rearrange("a d -> (a d)"))
                vector_rows(V_LNB, ins["o_ln_b_2"].rearrange("a d -> (a d)"))
                sp.dma_start(conv_rows[0:CONV_K * HALF, :],
                             ins["o_dw_2"].rearrange("a k (j c) -> (a k j) c", c=P)).then_inc(rows_landed, 16)
                sp.dma_start(log_dt[:, :], ins["o_log_dt_2"].rearrange("a (s g) -> (a s) g", g=2)).then_inc(ldt_landed, 16)
                sp.dma_start(sink[:, :, :].rearrange("p l h -> p (l h)"),
                             ins["sinks"].rearrange("l h -> (l h)").partition_broadcast(P)).then_inc(sink_landed, 16)

            def load(piece):
                if n[0] == RAW_RING:
                    small_inputs()
                if n[0] == 2 * RAW_RING:
                    sp.dma_start(const[:, FIRST_TABLES:], consts[:, FIRST_TABLES:]).then_inc(const_landed, 16)
                slot = n[0] % RAW_RING
                if n[0] >= RAW_RING:
                    piece_split(sp, n[0] - RAW_RING)
                sp.dma_start(raw[:, slot, :, 0:piece.shape[2]], piece).then_inc(raw_landed[slot], 16)
                n[0] += 1

            for l in range(DEPTH):
                for g in range(W_IN_GROUPS):
                    for half in range(2):
                        load(w_in_piece(l, g, half))
                for c in range(2):
                    load(square_piece(ins["w_a"][l], c, 0))
                for w in ("w_b", "w_out"):
                    for c in range(2):
                        for half in range(2):
                            load(square_piece(ins[w][l], c, half))
                for f in range(-2, F_GROUPS):
                    if l == DEPTH - 1 and f == 0:
                        for t in range(T):
                            sp.wait_ge(out_free[t], l * USES + USE_UP)
                        sp.dma_start(g_final, ins["g_final"].partition_broadcast(P)).then_inc(gfinal_landed, 16)
                        for b, w in enumerate(("o_b_re_2", "o_b_im_2")):
                            sp.dma_start(b_in[:, b, :, :], ins[w][0].rearrange("(s g) p i -> (g p) s i", g=2)).then_inc(s5_landed, 16)
                        for b, w in enumerate(("o_c_re_2", "o_c_im_2")):
                            sp.dma_start(c_in[:, b, :, :], ins[w][0].rearrange("(j g) o p -> (g o) j p", g=8)).then_inc(s5_landed, 16)
                    if f >= 0:
                        for c in range(2):
                            rows_f = ins["w_down"][l, f * COLS:(f + 1) * COLS, :]
                            load(square_piece(rows_f, c, 0))
                    if f + 2 < F_GROUPS:
                        for half in range(2):
                            load(square_piece(ins["w_up"][l], f + 2, half))
            for g in range(6):
                for half in range(2):
                    load(square_piece(ins["e_w_in_2"][0], (0, 1, 2, 4, 5, 3)[g], half))
                if g == 0:
                    sp.wait_ge(piece_used, E_PIECE)
                    sp.dma_start(pool_w[:, :, :], ins["e_pool_w_2"][0].rearrange("g c d -> c g d")).then_inc(poolw_landed, 16)
            for c in range(2):
                for half in (1, 0):
                    load(square_piece(ins["e_w_out_2"][0], c, half))
            sp.wait_ge(pv2_done, 2)
            sp.dma_start(g_post[0], ins["post_norm_g_2"][0].partition_broadcast(P)).then_inc(gpost_landed[0], 16)
            for g in range(5):
                for half in range(2):
                    load(square_piece(ins["o_w_in_2"][0], O_START[g] // COLS, half))
            for c in range(2):
                load(square_piece(ins["o_glu_w_2"][0], c, 0))
            load(square_piece(ins["o_pw_2"][0], 0, 0))
            for c in range(2):
                for half in range(2):
                    load(square_piece(ins["o_w_out_2"][0], c, half))
                if c == 0:
                    sp.wait_ge(states_ready, HALF)
                    sp.dma_start(g_post[1], ins["post_norm_g_2"][1].partition_broadcast(P)).then_inc(gpost_landed[1], 16)
            assert n[0] == ALL_PIECES
            for t in range(T):
                for half in range(2):
                    to = slice(half * COLS, (half + 1) * COLS)
                    sp.wait_ge(x_final, 2 * t + half + 1)
                    sp.dma_start(out[0, t * P:(t + 1) * P, to], x[:, t, to]).then_inc(stored, 16)
            sp.wait_ge(stored, 16 * 2 * T)

        @block.tensor
        def _(pe):
            def piece_ready(p):
                piece_split(pe, p)

            def out_ready(n, t):
                if n > 0:
                    pe.wait_ge(out_free[t], n)

            def products(parts, start, stop, shared=False, rows_hi=None, rows_lo=None):
                for i, (dst, a_hi, a_lo, b_hi, b_lo, rows_moving) in enumerate(parts):
                    first, last_one = start and i == 0, stop and i == len(parts) - 1
                    if rows_hi is not None:
                        rows_hi(i)
                    pe.matmul(dst, a_hi, b_hi, start=first, stop=False, skip_group_check=shared)
                    if rows_lo is None:
                        pe.matmul(dst, a_hi, b_lo, start=False, stop=False, skip_group_check=shared)
                        mm = pe.matmul(dst, a_lo, b_hi, start=False, stop=last_one, skip_group_check=shared)
                    elif rows_moving:
                        pe.matmul(dst, a_lo, b_hi, start=False, stop=False, skip_group_check=shared)
                    else:
                        pe.matmul(dst, a_hi, b_lo, start=False, stop=False, skip_group_check=shared)
                if rows_lo is not None:
                    for i, (dst, a_hi, a_lo, b_hi, b_lo, rows_moving) in enumerate(parts):
                        rows_lo(i)
                        last_one = stop and i == len(parts) - 1
                        if rows_moving:
                            mm = pe.matmul(dst, a_hi, b_lo, start=False, stop=last_one, skip_group_check=shared)
                        else:
                            mm = pe.matmul(dst, a_lo, b_hi, start=False, stop=last_one, skip_group_check=shared)
                return mm

            def rows_turned(turn, k0):
                def wait(ready):
                    return lambda i: pe.wait_ge(ready, 4 * turn + (k0 + i) // 2 + 1) if i % 2 == 0 else None
                return {"rows_hi": wait(turned_hi), "rows_lo": wait(turned_lo)}

            def tokens_out(n, p0, pieces, in_hi, in_lo, width=COLS, turn=None, halves=(0, 1), rows_ready=None, begin=0):
                for i in range(begin, pieces):
                    p = p0 + i
                    piece_ready(p)
                    if rows_ready is not None:
                        pe.wait_ge(cat_lo, rows_ready[i])
                    s = p % SPLIT_RING
                    for t in range(T):
                        if i == 0:
                            out_ready(n, t)
                        at = slice(t * P, (t + 1) * P)
                        k0 = halves[i] * KP
                        parts = [(OUT[t][:, 0:width], in_hi[:, k0 + kk, at], in_lo[:, k0 + kk, at],
                                  w_hi[:, s, kk, 0:width], w_lo[:, s, kk, 0:width], False) for kk in range(KP)]
                        waits = rows_turned(turn, k0) if turn is not None and t == 0 else {}
                        last = products(parts, i == 0, i == pieces - 1, **waits)
                        if t == 0 and i == pieces - 1:
                            last.then_inc(out0_done, 1)
                    last.then_inc(piece_used, 1)

            def features_out(n, p0, pieces, in_hi, in_lo, turn=None, after={}, banks=None):
                for i in range(pieces):
                    p = p0 + i
                    piece_ready(p)
                    s = p % SPLIT_RING
                    for j in range(HALF):
                        if i == 0 and j % 2 == 0 and banks is None:
                            out_ready(n, j // 2)
                        at = slice(j * P, (j + 1) * P)
                        dst = (banks or OUT)[j // 2][:, (j % 2) * SEQ:(j % 2 + 1) * SEQ]
                        parts = [(dst, w_hi[:, s, kk, at], w_lo[:, s, kk, at], in_hi[:, i * KP + kk, :],
                                  in_lo[:, i * KP + kk, :], True) for kk in range(KP)]
                        waits = rows_turned(turn, i * KP) if turn is not None and j == 0 else {}
                        last = products(parts, i == 0 and j % 2 == 0, i == pieces - 1, shared=True, **waits)
                        if j == 1 and i == pieces - 1:
                            last.then_inc(out0_done, 1)
                        if j < HALF - 1 and (i, j) in after:
                            after[i, j]()
                    last.then_inc(piece_used, 1)
                    if (i, HALF - 1) in after:
                        after[i, HALF - 1]()

            def keep_clock(b, n, m=ident):
                for _ in range(n):
                    pe.matmul(bank[:, b, 0:P], m, m, start=True, stop=True)

            def first_piece():
                parts = [(t, kk, slice(t * P, (t + 1) * P)) for kk in range(KP) for t in range(T)]
                pe.wait_ge(turned_hi, 2)
                for t, kk, at in parts:
                    if t == 0 and kk == 0:
                        pe.wait_ge(first_hi, 1)
                    if t == 0 and kk == KP // 2:
                        pe.wait_ge(hi_ready, 1)
                    pe.matmul(OUT[t], hT_hi[:, kk, at], w_hi[:, 0, kk, :], start=(kk == 0), stop=False)
                for t, kk, at in parts:
                    if t == 0 and kk == 0:
                        pe.wait_ge(first_lo, 1)
                    if t == 0 and kk == KP // 2:
                        piece_ready(0)
                    pe.matmul(OUT[t], hT_hi[:, kk, at], w_lo[:, 0, kk, :], start=False, stop=False)
                pe.wait_ge(turned_lo, 2)
                for t, kk, at in parts:
                    last = pe.matmul(OUT[t], hT_lo[:, kk, at], w_hi[:, 0, kk, :], start=False, stop=False)
                last.then_inc(piece_used, 1)

            def turn_rows(src, ready, need, groups=((0,), (1,), (2, 3))):
                for banks in groups:
                    for t in range(T):
                        for i in banks:
                            pe.wait_ge(ready(t), need(t, i))
                            for k in (2 * i, 2 * i + 1):
                                c = (k % 2) * SEQ + t * P
                                last = pe.transpose(ROWS_T[i][:, c:c + P], src[:, t, k * P:(k + 1) * P], ident)
                            if t == T - 1:
                                last.then_inc(turned, 1)

            pe.wait_ge(warm_zero, 1)
            keep_clock(2, WARM, h[:, 0, 0:P])
            pe.wait_ge(ident_landed, 16)
            pe.wait_ge(mix_landed, 16)
            pe.transpose(bank[:, 5, 0:V_MLP], rows[0:V_MLP, :], ident[0:V_MLP, 0:V_MLP]).then_inc(vec_turned, 1)

            def turn_vectors():
                pe.wait_ge(rows_landed, 16 * 10)
                pe.wait_ge(vec_ready, 1)
                pe.transpose(bank[:, 5, 0:V_ROWS], rows[0:V_ROWS, :], ident[0:V_ROWS, 0:V_ROWS]).then_inc(vec_turned, 1)
                pe.transpose(bank[:, 2, 0:CONV_K * HALF], conv_rows[0:CONV_K * HALF, :],
                             ident[0:CONV_K * HALF, 0:CONV_K * HALF]).then_inc(vec_turned, 1)
                pe.wait_ge(dt_spread, 1)
                pe.transpose(bank[:, 4, 0:S5_TILES], dt_rows[:, :, :].rearrange("s g p -> s (g p)"),
                             ident[0:S5_TILES, 0:S5_TILES]).then_inc(vec_turned, 1)

            def window(l, g):
                if l == 0 and g == 1:
                    turn_vectors()
                if g == 3:
                    if l == 0:
                        pe.wait_ge(vec_ready, 4)
                    for t in range(T):
                        pe.wait_ge(rot_done[t], l + 1)
                    for i in range(4):
                        for j in (2 * i, 2 * i + 1):
                            for t in range(T):
                                c = (j % 2) * SEQ + t * P
                                last = pe.transpose(TURN[i][:, c:c + P], z_ret[:, t, j * P:(j + 1) * P], ident)
                        last.then_inc(ret_turned, 1)
                if g == 4:
                    for t in range(T):
                        pe.wait_ge(rope_done[t], l + 1)
                    pe.wait_ge(rqT_ready, 2 * l + 1)
                    for b, src, n in ((2, z_att, 0), (5, z_att, 2), (3, ak_twice, 0)):
                        for j in range(2):
                            for t in range(T):
                                c = j * SEQ + t * P
                                last = pe.transpose(bank[:, b, c:c + P], src[:, t, (n + j) * P:(n + j + 1) * P], ident)
                        last.then_inc(att_turned, 1)
                if g == 5:
                    pe.wait_ge(rqT_ready, 2 * l + 2)
                    pe.wait_ge(rkT_ready, 2 * l + 2)
                    pe.wait_ge(akT_ready, l + 1)
                    for n in range(T):
                        at = slice(n * P, (n + 1) * P)
                        for hd in range(RET_HEADS):
                            last = pe.matmul(bank[:, 3 + n, hd * P:(hd + 1) * P], rkT[:, hd, at], rqT[:, hd, at],
                                             start=True, stop=True)
                        last.then_inc(s_ret_done, 1)
                    pe.wait_ge(aqT_first, l + 1)
                    pe.wait_ge(aqT_second, l + 1)
                if g == 6:
                    pe.wait_ge(s_ret_ready, 2 * l + 2)
                    pe.wait_ge(rkz_ready, l + 1)
                    for hd in range(RET_HEADS):
                        last = pe.matmul(bank[:, 3 + hd // 2, (hd % 2) * RET_V:(hd % 2 + 1) * RET_V],
                                         rk_zeta[:, hd * P:(hd + 1) * P], z_rv[:, 0, hd * RET_V:(hd + 1) * RET_V],
                                         start=True, stop=True)
                        if hd % 2:
                            last.then_inc(kv_done, 1)
                if 5 <= g < 5 + PAIRS:
                    i = g - 5
                    n = l * PAIRS + i
                    if n:
                        pe.wait_ge(scores_read, n)
                    heads = [(e, slice(e * HEAD, (e + 1) * HEAD), (2 * i + e) // (Q_HEADS // KV_HEADS)) for e in range(2)]
                    for e, rows_e, kv in heads:
                        pe.matmul(bank[:, 6 + e, 0:P], aqT[rows_e, i, 0:P], akT[rows_e, kv, 0:P], start=True, stop=True)
                    for e, rows_e, kv in heads:
                        last = pe.matmul(bank[:, 6 + e, P:3 * P], aqT[rows_e, i, P:SEQ], akT[rows_e, kv, :],
                                         start=True, stop=True)
                    last.then_inc(scores_done, 1)
                if 6 <= g < 6 + PAIRS:
                    n = l * PAIRS + g - 6
                    pe.wait_ge(probs_ready, n + 1)
                    if g > 6:
                        pe.wait_ge(probsT_even, n)
                        pe.wait_ge(probsT_odd, n)
                    for e in range(2):
                        for b in range(3):
                            last = pe.transpose(bank[:, (2, 5)[e], b * P:(b + 1) * P], probs[:, e, b * P:(b + 1) * P], ident)
                    last.then_inc(probs_turned, 1)
                if 7 <= g < 7 + PAIRS:
                    i = g - 7
                    n = l * PAIRS + i
                    pe.wait_ge(probsT_even, n + 1)
                    pe.wait_ge(probsT_odd, n + 1)
                    if i == 0:
                        pe.wait_ge(kv_ready, 2 * l + 2)
                    else:
                        pe.wait_ge(oT_lo, n)
                    for e in range(2):
                        kv = (2 * i + e) // (Q_HEADS // KV_HEADS)
                        v_at = slice(640 + kv * HEAD, 640 + (kv + 1) * HEAD)
                        dst = bank[e * HEAD:(e + 1) * HEAD, 3, :]
                        pe.matmul(dst[:, 0:P], z_att[:, 0, v_at], probsT[:, e, 0:P], start=True, stop=True)
                        pe.matmul(dst[:, P:SEQ], z_att[:, 0, v_at], probsT[:, e, P:2 * P], start=True, stop=False)
                        last = pe.matmul(dst[:, P:SEQ], z_att[:, 1, v_at], probsT[:, e, 2 * P:3 * P],
                                         start=False, stop=True)
                    last.then_inc(pv_done, 1)
                if g == 9:
                    pe.wait_ge(scores_read, l * PAIRS + PAIRS)
                    for hd in range(RET_HEADS):
                        last = pe.matmul(bank[:, 6 + hd // 2, (hd % 2) * RET_V:(hd % 2 + 1) * RET_V],
                                         s_ret[:, 0, hd * P:(hd + 1) * P], z_rv[:, 0, hd * RET_V:(hd + 1) * RET_V],
                                         start=True, stop=True)
                    last.then_inc(ret_done, 1)
                if g == 10:
                    pe.wait_ge(rqxi_ready, l + 1)
                    pe.wait_ge(probsT_even, l * PAIRS + PAIRS)
                    pe.wait_ge(probsT_odd, l * PAIRS + PAIRS)
                    for hd in range(RET_HEADS):
                        dst = bank[:, (2, 5)[hd // 2], (hd % 2) * RET_V:(hd % 2 + 1) * RET_V]
                        pe.matmul(dst, s_ret[:, 1, hd * P:(hd + 1) * P], z_rv[:, 1, hd * RET_V:(hd + 1) * RET_V],
                                  start=True, stop=False)
                        last = pe.matmul(dst, rqT_xi[:, hd, :], kv_state[:, hd, :], start=False, stop=True)
                    last.then_inc(ret_done, 1)

            def mlp_up(l, f):
                features_out(l * USES + USE_UP + f, l * PIECES + UP_PIECE[f], 2, hT_hi, hT_lo,
                             turn=4 * l + 3 if f == 0 else None)

            def mlp_down(l, f):
                pe.wait_ge(up_lo, 2 * (l * F_GROUPS + f + 1))
                for c in range(2):
                    p = l * PIECES + DOWN_PIECE[f] + c
                    piece_ready(p)
                    s = p % SPLIT_RING
                    for t in range(T):
                        at = slice(t * P, (t + 1) * P)
                        k0 = (f % 2) * HALF
                        parts = [(ACC[t][c], uT_hi[:, k0 + j, at], uT_lo[:, k0 + j, at], w_hi[:, s, j, :], w_lo[:, s, j, :], False)
                                 for j in range(HALF)]
                        last = products(parts, f == 0, f == F_GROUPS - 1)
                    last.then_inc(piece_used, 1)

            for l in range(DEPTH):
                if l == 0:
                    turn_rows(x, lambda t: x_landed[t], lambda t, i: 16)
                    keep_clock(2, WARM_WAIT)
                    first_piece()
                else:
                    turn_rows(x, lambda t: x_mlp, lambda t, i: 4 * (l - 1) + 2 * (i // 2) + t + 1)
                for g in range(W_IN_GROUPS):
                    tokens_out(l * USES + g, l * PIECES + 2 * g, 2, hT_hi, hT_lo,
                               width=AKV_WIDTH if g == AKV else COLS, turn=4 * l if g == 0 else None,
                               begin=1 if l == g == 0 else 0)
                    window(l, g)
                pe.wait_ge(oT_lo, PAIRS * (l + 1))
                for c in range(2):
                    tokens_out(l * USES + USE_YA + c, l * PIECES + PIECE_A + c, 1, uT_hi, uT_lo)
                turn_rows(h, lambda t: r_ready, lambda t, i: 2 * l + t + 1)
                for c in range(2):
                    tokens_out(l * USES + USE_YB + c, l * PIECES + PIECE_B + 2 * c, 2, hT_hi, hT_lo,
                               turn=4 * l + 1 if c == 0 else None)
                turn_rows(h, lambda t: m_ready, lambda t, i: 4 * l + 2 * (i // 2) + t + 1)
                for c in range(2):
                    tokens_out(l * USES + USE_O + c, l * PIECES + PIECE_O + 2 * c, 2, hT_hi, hT_lo,
                               turn=4 * l + 2 if c == 0 else None)
                turn_rows(x, lambda t: out_free[t], lambda t, i: l * USES + USE_O + i // 2 + 1)
                mlp_up(l, 0)
                mlp_up(l, 1)
                for f in range(F_GROUPS):
                    mlp_down(l, f)
                    if f + 2 < F_GROUPS:
                        mlp_up(l, f + 2)

            keep_clock(6, 24)
            turn_rows(h, lambda t: h_ready, lambda t, i: 2 * t + i // 2 + 1, groups=(range(4),))
            for g in range(3):
                tokens_out(E_USE + g, E_PIECE + 2 * g, 2, hT_hi, hT_lo, turn=4 * DEPTH if g == 0 else None)
            pe.wait_ge(rope2_done, 2 * T)
            for i in range(4):
                for j in (2 * i, 2 * i + 1):
                    for t in range(T):
                        c = (j % 2) * SEQ + t * P
                        src = (zq, zk)[j // ATT2_HEADS][:, t, (j % ATT2_HEADS) * P:(j % ATT2_HEADS + 1) * P]
                        last = pe.transpose(TURN[i][:, c:c + P], src, ident)
                last.then_inc(qk2_turned, 1)
            features_out(E_USE + 3, E_PIECE + 6, 2, hT_hi, hT_lo)
            pe.wait_ge(q2T_ready, 2)
            pe.wait_ge(k2T_ready, 2)
            for hd in range(ATT2_HEADS):
                pe.matmul(TURN[hd][:, 0:P], q2T[:, hd, 0:P], k2T[:, hd, 0:P], start=True, stop=True)
                last = pe.matmul(TURN[hd][:, P:3 * P], q2T[:, hd, P:SEQ], k2T[:, hd, :], start=True, stop=True)
                last.then_inc(scores2_done, 1)
            features_out(E_USE + 4, E_PIECE + 8, 2, hT_hi, hT_lo)
            for hd in range(ATT2_HEADS):
                pe.wait_ge(probs2_ready, hd + 1)
                for b in range(3):
                    last = pe.transpose(TURN[hd][:, b * P:(b + 1) * P], probs2[:, hd, b * P:(b + 1) * P], ident)
                last.then_inc(probs2_turned, 1)
            pe.wait_ge(pool_mean, 1)
            pe.wait_ge(poolw_landed, 16)
            for j in range(HALF):
                last = pe.matmul(bank[:, (2, 5)[j // 2], (j % 2) * SEQ:(j % 2 + 1) * SEQ], pool_w[:, j, :], pool_m[:, j, :],
                                 start=True, stop=True)
                if j % 2:
                    last.then_inc(pool_done, 1)

            def values2():
                pe.wait_ge(probs2T_act, 2)
                pe.wait_ge(probs2T_dve, 2)
                for hd in range(ATT2_HEADS):
                    dst = TURN[hd // 2][:, (hd % 2) * SEQ:(hd % 2 + 1) * SEQ]
                    v_at = slice(hd * P, (hd + 1) * P)
                    pe.matmul(dst[:, 0:P], zv[:, 0, v_at], probs2T[:, hd, 0:P], start=True, stop=True)
                    pe.matmul(dst[:, P:SEQ], zv[:, 0, v_at], probs2T[:, hd, P:2 * P], start=True, stop=False)
                    last = pe.matmul(dst[:, P:SEQ], zv[:, 1, v_at], probs2T[:, hd, 2 * P:3 * P], start=False, stop=True)
                    if hd % 2:
                        last.then_inc(pv2_done, 1)

            features_out(E_USE + 5, E_PIECE + 10, 2, hT_hi, hT_lo, after={(0, HALF - 1): values2})
            for c in range(2):
                tokens_out(E_OUT_USE + c, E_OUT_PIECE + 2 * c, 2, uT_hi, uT_lo, halves=(1, 0), rows_ready=(2, 4))
            pe.wait_ge(s5_padded, 8)
            for b in range(2):
                for j in range(HALF):
                    last = pe.transpose(bank[:, 2 + 3 * b, j * P:(j + 1) * P],
                                        b_pad[:, b, 4 * j:4 * j + 4, :].rearrange("p s i -> p (s i)"), ident)
                last.then_inc(s5_turned, 1)
            for b in range(2):
                for j in range(HALF):
                    last = pe.transpose(bank[:, 6 + b, j * P:(j + 1) * P], c_pad[:, b, j, :], ident)
                last.then_inc(s5_turned, 1)

            keep_clock(3, 20)
            pe.wait_ge(s5_mats, 3)
            turn_rows(h, lambda t: h_ready, lambda t, i: 2 * T + 2 * t + i // 2 + 1, groups=(range(4),))
            def drive(j, b):
                if j == 0:
                    pe.wait_ge(s5_mats, 5)
                    for t in range(2):
                        pe.wait_ge(out_free[t], O_USE + SU + 1)
                else:
                    pe.wait_ge(drive_read, j)
                for q in range(4):
                    rows_q = slice(32 * q, 32 * q + 32)
                    last = pe.matmul(bank[:, 4 + q, b * SEQ:(b + 1) * SEQ], b_mat[rows_q, b, j, :], su[rows_q, j, :],
                                     start=True, stop=True)
                if b == 1:
                    last.then_inc(drive_done, 1)

            def outputs(j):
                pe.wait_ge(states_ready, j + 1)
                if j:
                    pe.wait_ge(y_ready, j)
                for q in range(4):
                    dst = bank[32 * q:32 * q + 32, 2, 0:SEQ]
                    parts = (s5_x[j % 2][0], s5_o[1], s5_o[0], s5_x[j % 2][1])
                    for i, m in enumerate((0, 1, 2, 2)):
                        last = pe.matmul(dst, c_mat[:, m, j, 32 * q:32 * q + 32], parts[i][:, q, :],
                                         start=(i == 0), stop=(i == 3))
                last.then_inc(y_done, 1)

            def convolve(n0, n1):
                pe.wait_ge(conv_gated, 1)
                for n in range(n0, n1):
                    j, k = divmod(n, CONV_K)
                    chunk, i = divmod(n, CHUNK)
                    if i == 0 or n == n0:
                        pe.wait_ge(conv_diag_ready, chunk + 1)
                    mm = pe.matmul(bank[:, 3, j * SEQ:(j + 1) * SEQ], conv_diag[:, (chunk % 2) * CHUNK + i, :],
                                   conv_in[:, j, k:k + SEQ], start=(n == 0), stop=(k == CONV_K - 1), skip_group_check=True)
                    if i == CHUNK - 1 or n == PE_CONV * CONV_K - 1:
                        mm.then_inc(conv_used, 1)

            features_out(O_USE + SU, O_PIECE + 2 * SU, 2, hT_hi, hT_lo, turn=4 * DEPTH + 1)
            features_out(O_USE + CA, O_PIECE + 2 * CA, 2, hT_hi, hT_lo, after={(0, 1): lambda: drive(0, 0), (0, 3): lambda: drive(0, 1)})
            features_out(O_USE + CB, O_PIECE + 2 * CB, 2, hT_hi, hT_lo, after={(0, 1): lambda: drive(1, 0), (0, 3): lambda: drive(1, 1)})
            features_out(O_USE + GC, O_PIECE + 2 * GC, 2, hT_hi, hT_lo, after={(0, 1): lambda: drive(2, 0), (0, 2): lambda: drive(2, 1), (0, 3): lambda: outputs(0)})
            features_out(O_USE + GD, O_PIECE + 2 * GD, 2, hT_hi, hT_lo, after={(0, 2): lambda: outputs(1), (0, 3): lambda: drive(3, 0), (1, 0): lambda: drive(3, 1)})
            convolve(0, CHUNK)
            outputs(2)
            convolve(CHUNK, 4 * CHUNK)
            outputs(3)
            convolve(4 * CHUNK, PE_CONV * CONV_K)
            pe.wait_ge(conv_taken, 1)
            pe.wait_ge(conv_done, HALF - PE_CONV)
            for t in range(T):
                for j in range(HALF):
                    last = pe.transpose(bank[:, 4 + t, j * P:(j + 1) * P], conv_out[:, j, t * P:(t + 1) * P], ident)
                last.then_inc(conv_turned, 1)
            pe.wait_ge(y_lo, HALF)
            features_out(GLU_USE, GLU_PIECE, 1, hT_hi, hT_lo)
            pe.wait_ge(ln_done, T)
            for j in range(HALF):
                for t in range(T):
                    c = (j % 2) * SEQ + t * P
                    last = pe.transpose(bank[:, 6 + j // 2, c:c + P], conv_tok[:, t, j * P:(j + 1) * P], ident)
                if j % 2:
                    last.then_inc(ln_turned, 1)
            features_out(GLU_USE + 1, GLU_PIECE + 1, 1, hT_hi, hT_lo)
            pe.wait_ge(cat_lo, 4 + 2)
            features_out(PW_USE, PW_PIECE, 1, hT_hi[:, HALF:KD, :], hT_lo[:, HALF:KD, :], banks=PW_BANKS)
            for c in range(2):
                tokens_out(O_OUT_USE + c, O_OUT_PIECE + 2 * c, 2, uT_hi, uT_lo, rows_ready=(4 + 2 + 2, 4 + 2 + 4))

        @block.scalar
        def _(act):
            order = Order(act, act_order)
            copy = ACT.Copy

            def split(p):
                if p >= ALL_PIECES:
                    return
                n = AKV_WIDTH if p < DEPTH * PIECES and p % PIECES in (2 * AKV, 2 * AKV + 1) else COLS
                act.wait_ge(raw_landed[p % RAW_RING], 16 * (p // RAW_RING + 1))
                if p >= SPLIT_RING:
                    act.wait_ge(piece_used, p - SPLIT_RING + 1)
                act.activation(w_hi[:, p % SPLIT_RING, :, 0:n], raw[:, p % RAW_RING, :, 0:n], copy).then_inc(hi_ready, 1)

            def step(p):
                split(p + AHEAD)

            def evacuate(n, dst, func=copy, scale=None, between=None):
                for t in range(2):
                    if t and between is not None:
                        between()
                    whole(act, n, t)
                    d = dst(t)
                    act.activation(d, OUT[t][:, 0:int(np.prod(d.shape[1:]))] if len(d.shape) == 2 else
                                   OUT[t].rearrange("p (a b) -> p a b", b=d.shape[2]),
                                   func, scale=1.0 if scale is None else scale(t)).then_inc(out_free[t], 1)

            def squares(n, t, c):
                act.activation(h[:, t, c * COLS:(c + 1) * COLS], x[:, t, c * COLS:(c + 1) * COLS], ACT.Square, scale=D ** -0.5,
                               accum_out=ssq[:, n, t, c:c + 1]).then_inc(sq_done[t], 1)

            def turn_hi(ph, gain=None, scale=1.0, banks=range(4)):
                for i in banks:
                    act.wait_ge(turned, 4 * ph + i + 1)
                    if gain is None:
                        last = act.activation(hT_hi[:, 2 * i:2 * i + 2, :].rearrange("p k t -> p (k t)"), ROWS_T[i], copy, scale=scale)
                    else:
                        for k in (2 * i, 2 * i + 1):
                            last = act.activation(hT_hi[:, k, :], ROWS_T[i][:, (k % 2) * SEQ:(k % 2 + 1) * SEQ], copy,
                                                  scale=vec[:, gain + k:gain + k + 1])
                    last.then_inc(turned_hi, 1)

            act.dma_start(const[:, 0:FIRST_TABLES], consts[:, 0:FIRST_TABLES]).then_inc(ident_landed, 16)
            act.dma_start(rows[V_MIX:V_MLP, :], ins["g_mix"].rearrange("l (r c) -> (l r) c", c=P)).then_inc(mix_landed, 16)
            act.wait_ge(vec_turned, 1)
            act.activation(vec[:, 0:V_MLP], bank[:, 5, 0:V_MLP], copy).then_inc(vec_ready, 1)
            act.wait_ge(vec_ready, 1)
            turn_hi(0, gain=V_MIX, banks=range(2))
            act.wait_ge(raw_landed[0], 16)
            for half, done in ((0, first_hi), (1, hi_ready)):
                k = slice(half * KP // 2, (half + 1) * KP // 2)
                act.activation(w_hi[:, 0, k, :], raw[:, 0, k, :], copy).then_inc(done, 1)
            split(1)
            turn_hi(0, gain=V_MIX, banks=range(2, 4))
            for t in range(T):
                act.wait_ge(x_landed[t], 16)
                for c in range(2):
                    squares(0, t, c)

            def vectors_turned():
                act.wait_ge(vec_turned, 4)
                act.activation(vec[:, V_MLP:], bank[:, 5, V_MLP:V_ROWS], copy).then_inc(vec_ready, 1)
                act.activation(conv_w[:, :, :].rearrange("p k j -> p (k j)"), bank[:, 2, 0:CONV_K * HALF], copy).then_inc(vec_ready, 1)
                act.activation(s5_dt[:, :], bank[:, 4, 0:S5_TILES], ACT.Exp).then_inc(vec_ready, 1)
                act.wait_ge(vec_ready, 4)

            def window(l, g):
                if l == 0 and g == 1:
                    vectors_turned()
                if g == 3:
                    for i in range(2):
                        act.wait_ge(ret_turned, 4 * l + i + 1)
                        act.activation(rqT[:, 2 * i:2 * i + 2, :].rearrange("p h t -> p (h t)"), TURN[i], copy)\
                           .then_inc(rqT_ready, 1)
                if g == 4:
                    act.wait_ge(att_turned, 3 * l + 1)
                    act.activation(aqT[:, 0:2, :].rearrange("p i t -> p (i t)"), bank[:, 2, :], copy).then_inc(aqT_first, 1)
                    act.wait_ge(att_turned, 3 * l + 3)
                    act.activation(akT[:, :, :].rearrange("p i t -> p (i t)"), bank[:, 3, :], copy).then_inc(akT_ready, 1)
                if g == 6:
                    for b in range(2):
                        act.wait_ge(kv_done, 2 * l + b + 1)
                        act.activation(kv_state[:, 2 * b:2 * b + 2, :].rearrange("p h e -> p (h e)"), bank[:, 3 + b, :], copy)\
                           .then_inc(kv_ready, 1)
                if 6 <= g < 6 + PAIRS:
                    n = l * PAIRS + g - 6
                    act.wait_ge(probs_turned, n + 1)
                    if n:
                        act.wait_ge(pv_done, n)
                    act.activation(probsT[:, 0, :], bank[:, 2, 0:384], copy).then_inc(probsT_even, 1)
                if 7 <= g < 7 + PAIRS:
                    i = g - 7
                    act.wait_ge(pv_done, l * PAIRS + i + 1)
                    act.activation(uT_hi[:, i, :], bank[:, 3, 0:SEQ], copy).then_inc(oT_hi, 1)
                if 5 <= g < 5 + PAIRS:
                    n = l * PAIRS + g - 5
                    act.wait_ge(top_ready, n + 1)
                    for e in range(2):
                        for t in range(T):
                            p_at = probs[:, e, 0:P] if t == 0 else probs[:, e, P:3 * P]
                            act.activation(p_at, p_at, ACT.Exp, bias=neg_top[:, e, t:t + 1], accum_out=den[:, e, t:t + 1])
                    act.activation(sink_exp[:, :, :], sink_gap[:, :, :], ACT.Exp).then_inc(exp_done, 1)
                if g in (9, 10):
                    t = g - 9
                    act.wait_ge(ret_done, 2 * l + t + 1)
                    for hd in range(RET_HEADS):
                        src = bank[:, ((6, 7), (2, 5))[t][hd // 2], (hd % 2) * RET_V:(hd % 2 + 1) * RET_V]
                        last = act.activation(h[:, t, hd * RET_V:(hd + 1) * RET_V], src, ACT.Square,
                                              accum_out=ret_ss[:, t, hd:hd + 1])
                    last.then_inc(ret_sq, 1)

            def group_out(l, g):
                n = l * USES + g

                def full(t):
                    return rstd[:, 2 * l, t:t + 1]

                def half(t):
                    return half_rstd[:, l, t:t + 1]

                if g == RQ:
                    act.wait_ge(rstd_ready, stat_count(2 * l, T - 1))
                    act.wait_ge(half_ready, l + 1)
                    evacuate(n, lambda t: z_ret[:, t, 0:512], scale=full, between=lambda: step(l * PIECES + 2 * g + 1))
                elif g == RK:
                    evacuate(n, lambda t: z_ret[:, t, 512:1024], scale=full)
                elif g == AQ:
                    evacuate(n, lambda t: z_att[:, t, 0:512], scale=full)
                elif g == AKV:
                    evacuate(n, lambda t: z_att[:, t, 512:768], scale=full)
                elif g in (RV0, RV1):
                    evacuate(n, lambda t: z_rv[:, t, (g - RV0) * COLS:(g - RV0 + 1) * COLS], scale=full)
                elif g in (RG0, RG1):
                    for t in range(T):
                        whole(act, n, t)
                        act.activation(rg_tanh[:, t, :], OUT[t], ACT.Tanh, scale=half(t)).then_inc(tanh_ready, 1)
                elif g in (GA0, GA1):
                    evacuate(n, lambda t: z_ga[:, t, (g - GA0) * COLS:(g - GA0 + 1) * COLS], ACT.Tanh, scale=half)
                else:
                    evacuate(n, lambda t: z_gb[:, t, (g - GB0) * COLS:(g - GB0 + 1) * COLS], ACT.Tanh, scale=half)

            def mlp_square(l, f):
                n = l * USES + USE_UP + f
                for b in range(2):
                    m = 2 * (l * F_GROUPS + f) + b
                    whole(act, n, b)
                    if f >= 2:
                        act.wait_ge(piece_used, l * PIECES + DOWN_PIECE[f - 2] + 2)
                    if m >= 2:
                        act.wait_ge(up_lo, m - 1)
                    act.activation(relu_buf[:, b, :], OUT[b], ACT.Relu).then_inc(out_free[b], 1)
                    act.wait_ge(out_free[b], n + 1)
                    k = (f % 2) * HALF + 2 * b
                    act.activation(uT_hi[:, k:k + 2, :].rearrange("p k t -> p (k t)"), relu_buf[:, b, :], ACT.Square)\
                       .then_inc(up_hi, 1)

            for l in range(DEPTH):
                p = l * PIECES
                if l:
                    turn_hi(4 * l, gain=V_MIX + KD * l)
                    for t in range(T):
                        squares(2 * l, t, 1)
                for g in range(W_IN_GROUPS):
                    step(p + 2 * g)
                    window(l, g - 1)
                    if g != RQ:
                        step(p + 2 * g + 1)
                    group_out(l, g)
                step(p + PIECE_A)
                step(p + PIECE_A + 1)
                turn_hi(4 * l + 1)
                for i in range(4):
                    step(p + PIECE_B + i)
                turn_hi(4 * l + 2, scale=0.5)
                for c in range(2):
                    step(p + PIECE_O + 2 * c)
                    step(p + PIECE_O + 2 * c + 1)
                    if c == 1:
                        turn_hi(4 * l + 3, gain=V_MLP + KD * l)
                    for t in range(T):
                        act.wait_ge(out_free[t], l * USES + USE_O + c + 1)
                        squares(2 * l + 1, t, c)
                for f in range(2):
                    step(p + UP_PIECE[f])
                    step(p + UP_PIECE[f] + 1)
                    mlp_square(l, f)
                for f in range(F_GROUPS):
                    step(p + DOWN_PIECE[f])
                    step(p + DOWN_PIECE[f] + 1)
                    if f + 2 < F_GROUPS:
                        step(p + UP_PIECE[f + 2])
                        step(p + UP_PIECE[f + 2] + 1)
                        mlp_square(l, f + 2)
                for c in range(2 if l == DEPTH - 1 else 1):
                    for t in range(T):
                        act.wait_ge(x_mlp, 4 * l + 2 * c + t + 1)
                        squares(2 * l + 2, t, c)
                        if l == DEPTH - 1:
                            act.wait_ge(xg_ready, 2 * c + t + 1)
                            act.activation(final_junk[:, 2 * t + c, :], xg[:, t, c * COLS:(c + 1) * COLS], ACT.Square, scale=D ** -0.5,
                                           accum_out=ssq[:, 2 * DEPTH + 1, t, c:c + 1]).then_inc(sq_done[t], 1)

            turn_hi(4 * DEPTH, gain=V_PRE)
            p = E_PIECE
            step(p)
            act.wait_ge(s5_decay_in, 1)
            act.activation(s5_small[:, 2, :], s5_small[:, 0, :], ACT.Exp).then_inc(s5_decay, 1)
            act.wait_ge(s5_angles, 1)
            act.activation(s5_sin[:, :, :].rearrange("p s t -> p (s t)"), s5_sin[:, :, :].rearrange("p s t -> p (s t)"),
                           ACT.Sin, scale=TWO_PI).then_inc(s5_tables, 1)
            step(p + 1)
            act.wait_ge(final_scaled, T)
            evacuate(E_USE, lambda t: zq[:, t, :])
            step(p + 2)
            act.activation(s5_cos[:, :, :].rearrange("p s t -> p (s t)"), s5_cos[:, :, :].rearrange("p s t -> p (s t)"),
                           ACT.Sin, scale=TWO_PI).then_inc(s5_tables, 1)
            step(p + 3)
            evacuate(E_USE + 1, lambda t: zk[:, t, :])
            step(p + 4)
            step(p + 5)
            evacuate(E_USE + 2, lambda t: zv[:, t, :])
            step(p + 6)
            for i in range(2):
                act.wait_ge(qk2_turned, i + 1)
                act.activation(q2T[:, 2 * i:2 * i + 2, :].rearrange("p h t -> p (h t)"), TURN[i], copy).then_inc(q2T_ready, 1)
            step(p + 7)
            act.wait_ge(pool_zero, 1)
            evacuate(E_USE + 3, lambda t: pool_in[:, 2 * t:2 * t + 2, POOL_PAD:PW])
            step(p + 8)
            for hd in range(ATT2_HEADS):
                act.wait_ge(top2_ready, hd + 1)
                for t in range(T):
                    p_at = probs2[:, hd, 0:P] if t == 0 else probs2[:, hd, P:3 * P]
                    last = act.activation(p_at, p_at, ACT.Exp, bias=neg_top2[:, hd, t:t + 1], accum_out=den2[:, hd, t:t + 1])
                last.then_inc(exp2_done, 1)
            step(p + 9)
            evacuate(E_USE + 4, lambda t: gate_b[:, 2 * t:2 * t + 2, :], ACT.Silu)
            step(p + 10)
            for hd in range(2):
                act.wait_ge(probs2_turned, hd + 1)
                act.activation(probs2T[:, hd, :], TURN[hd][:, 0:384], copy).then_inc(probs2T_act, 1)

            def cat_upper(ready, count, dst, src):
                act.wait_ge(ready, count)
                act.activation(dst, src, copy).then_inc(cat_hi, 1)

            for i in (2, 3):
                cat_upper(cat_tmp_ready, i - 1, uT_hi[:, 2 * i:2 * i + 2, :], mix_tmp[:, 2 * i:2 * i + 2, :])
            step(p + 11)
            evacuate(E_USE + 5, lambda t: gate_a[:, 2 * t:2 * t + 2, :], ACT.Silu)
            for i in (0, 1):
                cat_upper(cat_tmp_ready, 2 + i + 1, uT_hi[:, 2 * i:2 * i + 2, :], mix_tmp[:, 2 * i:2 * i + 2, :])

            def post_squares(norm, n, piece, late=()):
                for c in range(2):
                    for i in ((0,), (1, 2, 3))[c]:
                        if piece + i + AHEAD not in late:
                            step(piece + i)
                    for t in range(T):
                        whole(act, n + c, t)
                        act.activation(sq_junk[:, 2 * t + c, :], OUT[t], ACT.Square, scale=D ** -0.5,
                                       accum_out=ssq[:, norm, t, c:c + 1]).then_inc(sq_done[t], 1)

            post_squares(2 * DEPTH + 2, E_OUT_USE, E_OUT_PIECE)
            for c in range(2):
                act.wait_ge(post_ready, c + 1)
                squares(2 * DEPTH + 3, 0, c)
            act.wait_ge(s5_turned, 4)
            act.activation(c_mat[:, 0, :, :].rearrange("p j c -> p (j c)"), bank[:, 6, :], copy).then_inc(s5_mats, 1)
            act.activation(c_mat[:, 1, :, :].rearrange("p j c -> p (j c)"), bank[:, 6, :], copy, scale=-1.0).then_inc(s5_mats, 1)
            act.activation(c_mat[:, 2, :, :].rearrange("p j c -> p (j c)"), bank[:, 7, :], copy, scale=-1.0).then_inc(s5_mats, 1)
            for c in range(2):
                act.wait_ge(post_ready, 2 + c + 1)
                squares(2 * DEPTH + 3, 1, c)
            act.activation(b_mat[:, 0, :, :].rearrange("p j c -> p (j c)"), bank[:, 2, :], copy).then_inc(s5_mats, 1)
            act.activation(b_mat[:, 1, :, :].rearrange("p j c -> p (j c)"), bank[:, 5, :], copy).then_inc(s5_mats, 1)
            turn_hi(4 * DEPTH + 1, gain=V_PRE + KD)
            p = O_PIECE
            step(p + 2 * SU)
            evacuate(O_USE + SU, lambda t: su[:, 2 * t:2 * t + 2, :], between=lambda: step(O_PIECE + 2 * SU + 1))
            step(p + 2 * CA)
            step(p + 2 * CA + 1)
            act.wait_ge(conv_zero, 1)
            evacuate(O_USE + CA, lambda t: conv_in[:, 2 * t:2 * t + 2, CONV_K - 1:CW])
            step(p + 2 * CB)
            step(p + 2 * CB + 1)
            evacuate(O_USE + CB, lambda t: gate_d[:, 2 * t:2 * t + 2, :], ACT.Sigmoid)
            step(p + 2 * GC)
            step(p + 2 * GC + 1)
            evacuate(O_USE + GC, lambda t: gate_c[:, 2 * t:2 * t + 2, :], ACT.Silu)
            step(p + 2 * GD)
            step(p + 2 * GD + 1)

            def conv_diagonals(chunk):
                act.wait_ge(conv_used, chunk - 1)
                for i in range(CHUNK):
                    j, k = divmod(chunk * CHUNK + i, CONV_K)
                    if j < PE_CONV:
                        last = act.activation(conv_diag[:, (chunk % 2) * CHUNK + i, :], ident, copy, scale=conv_w[:, k, j:j + 1])
                last.then_inc(conv_diag_ready, 1)

            def y_upper(j):
                act.wait_ge(y_ready, j + 1)
                act.activation(hT_hi[:, j, :], y_ssm[:, j, :], copy).then_inc(cat_hi, 1)

            act.wait_ge(conv_gated, 1)
            evacuate(O_USE + GD, lambda t: gate_d[:, 2 * t:2 * t + 2, :], ACT.Silu)
            step(GLU_PIECE)
            y_upper(0)
            y_upper(1)
            conv_diagonals(2)
            conv_diagonals(3)
            y_upper(2)
            conv_diagonals(4)
            conv_diagonals(5)
            y_upper(3)
            act.wait_ge(conv_used, CHUNKS)
            act.activation(conv_out[:, 0:PE_CONV, :].rearrange("p j t -> p (j t)"), bank[:, 3, :], copy).then_inc(conv_taken, 1)

            def glu_gate():
                for b in range(2):
                    whole(act, GLU_USE + 1, b)
                    for j in (2 * b, 2 * b + 1):
                        last = act.activation(glu_s[:, j, :], OUT[b][:, (j % 2) * SEQ:(j % 2 + 1) * SEQ], ACT.Sigmoid,
                                              bias=vec[:, V_GLUB + HALF + j:V_GLUB + HALF + j + 1])
                    last.then_inc(out_free[b], 1)

            step(GLU_PIECE + 1)
            for b in range(2):
                act.wait_ge(ln_turned, b + 1)
                for j in (2 * b, 2 * b + 1):
                    last = act.activation(conv_act[:, j, :], bank[:, 6 + b, (j % 2) * SEQ:(j % 2 + 1) * SEQ], ACT.Silu,
                                          scale=vec[:, V_LNG + j:V_LNG + j + 1], bias=vec[:, V_LNB + j:V_LNB + j + 1])
                last.then_inc(conv_silu, 1)
                act.wait_ge(conv_silu, b + 1)
                act.activation(hT_hi[:, HALF + 2 * b:HALF + 2 * b + 2, :], conv_act[:, 2 * b:2 * b + 2, :], copy).then_inc(cat_hi, 1)
            glu_gate()
            for i in range(2):
                cat_upper(cat_tmp_ready, 4 + i + 1, uT_hi[:, 2 * i:2 * i + 2, :], cat_tmp[:, 2 * i:2 * i + 2, :])
            step(PW_PIECE)
            for i in range(2, 4):
                cat_upper(out_free[i - 2], PW_USE + 1, uT_hi[:, 2 * i:2 * i + 2, :], cat_tmp[:, 2 * i:2 * i + 2, :])
            step(O_OUT_PIECE)
            post_squares(2 * DEPTH + 4, O_OUT_USE, O_OUT_PIECE, late=(O_OUT_PIECE + 2,))

        @block.vector
        def _(dve):
            order = Order(dve, dve_order)

            def split(p):
                if p >= ALL_PIECES or p in POOL_PIECES:
                    return
                n = AKV_WIDTH if p < DEPTH * PIECES and p % PIECES in (2 * AKV, 2 * AKV + 1) else COLS
                s = p % SPLIT_RING
                dve.wait_ge(hi_ready, p + 1)
                dve.tensor_tensor(w_lo[:, s, :, 0:n], raw[:, p % RAW_RING, :, 0:n], w_hi[:, s, :, 0:n].bitcast(F32),
                                  ALU.subtract).then_inc(lo_ready, 1)

            def step(p):
                split(p + AHEAD)

            def row_mean(n, t):
                dve.wait_ge(sq_done[t], 2 * n + 2)
                dve.scalar_tensor_tensor(out=mean[:, n, t:t + 1], in0=ssq[:, n, t, 0:1], scalar=EPS, in1=ssq[:, n, t, 1:2],
                                         op0=ALU.add, op1=ALU.add).then_inc(mean_ready, 1)

            def row_scale(n, t):
                row_mean(n, t)
                dve.wait_ge(rstd_ready, stat_count(n, t))

            def turn_lo(ph, gain=None, scale=1.0, banks=range(4)):
                for i in banks:
                    dve.wait_ge(turned_hi, 4 * ph + i + 1)
                    for k in (2 * i, 2 * i + 1):
                        last = dve.scalar_tensor_tensor(
                            out=hT_lo[:, k, :], in0=ROWS_T[i][:, (k % 2) * SEQ:(k % 2 + 1) * SEQ],
                            scalar=scale if gain is None else vec[:, gain + k:gain + k + 1],
                            in1=hT_hi[:, k, :].bitcast(F32), op0=ALU.mult, op1=ALU.subtract)
                    last.then_inc(turned_lo, 1)

            dve.memset(h[:, 0, 0:P], 0.0).then_inc(warm_zero, 1)
            dve.wait_ge(vec_ready, 1)
            turn_lo(0, gain=V_MIX, banks=range(2))
            for half, upper, done in ((0, first_hi, first_lo), (1, hi_ready, lo_ready)):
                k = slice(half * KP // 2, (half + 1) * KP // 2)
                dve.wait_ge(upper, 1)
                dve.tensor_tensor(w_lo[:, 0, k, :], raw[:, 0, k, :], w_hi[:, 0, k, :].bitcast(F32), ALU.subtract).then_inc(done, 1)
            split(1)
            turn_lo(0, gain=V_MIX, banks=range(2, 4))
            dve.wait_ge(ldt_landed, 16)
            dve.tensor_copy(dt_rows[:, :, :], log_dt[:, :].unsqueeze(2).broadcast_to([S5_TILES, 2, S5_STATE]))\
               .then_inc(dt_spread, 1)

            def softmax(l, i):
                n = l * PAIRS + i
                dve.wait_ge(scores_done, n + 1)
                if n:
                    dve.wait_ge(probs_turned, n)
                for e in range(2):
                    ins_ = dve.scalar_tensor_tensor(out=probs[:, e, :], in0=bank[:, 6 + e, 0:384], scalar=float(HEAD) ** -0.5,
                                                    in1=tab("window"), op0=ALU.mult, op1=ALU.add)
                    if e == 0:
                        order.mark(ins_)
                ins_.then_inc(scores_read, 1)
                order.settle()
                dve.wait_ge(scores_read, n + 1)
                order.mark(dve.tensor_reduce(top[:, :, 0], probs[:, :, 0:P], AX_X, ALU.max))
                order.link(dve.tensor_reduce(top[:, :, 1], probs[:, :, P:3 * P], AX_X, ALU.max))
                s = sink[:, l, 2 * i:2 * i + 2].unsqueeze(2).broadcast_to([P, 2, T])
                order.link(dve.tensor_tensor(top[:, :, :], top[:, :, :], s, ALU.max))
                order.mark(dve.tensor_scalar(neg_top[:, :, :], top[:, :, :], -1.0, None, ALU.mult))
                dve.tensor_tensor(sink_gap[:, :, :], s, top[:, :, :], ALU.subtract).then_inc(top_ready, 1)
                dve.wait_ge(exp_done, n + 1)
                order.link(dve.tensor_tensor(den_all[:, :, :], den[:, :, :], sink_exp[:, :, :], ALU.add))
                order.link(dve.reciprocal(inv_den[:, :, :], den_all[:, :, :]))
                for e in range(2):
                    for t in range(T):
                        p_at = probs[:, e, 0:P] if t == 0 else probs[:, e, P:3 * P]
                        last = dve.tensor_scalar(p_at, p_at, inv_den[:, e, t:t + 1], None, ALU.mult)
                last.then_inc(probs_ready, 1)

            def retention_out(l, t):
                dve.wait_ge(ret_sq, 2 * l + t + 1)
                dve.tensor_scalar(ret_ms[:, t, :], ret_ss[:, t, :], 4.0 / RET_V, 4.0 * EPS, ALU.mult, ALU.add).then_inc(ret_mean, 1)
                dve.wait_ge(ret_scale, 2 * l + t + 1)
                for hd in range(RET_HEADS):
                    at = slice(hd * RET_V, (hd + 1) * RET_V)
                    src = bank[:, ((6, 7), (2, 5))[t][hd // 2], (hd % 2) * RET_V:(hd % 2 + 1) * RET_V]
                    last = dve.scalar_tensor_tensor(out=h[:, t, at], in0=src, scalar=ret_rstd[:, t, hd:hd + 1],
                                                    in1=z_rg[:, t, at], op0=ALU.mult, op1=ALU.mult)
                last.then_inc(r_ready, 1)

            def window(l, g):
                if g == 1:
                    dve.wait_ge(const_landed, 16)
                    dve.wait_ge(sink_landed, 16)
                    dve.wait_ge(vec_ready, 4)
                    rotate_pairs(dve, order, l, 0, z_ga)
                if g == 3:
                    for i in range(2, 4):
                        dve.wait_ge(ret_turned, 4 * l + i + 1)
                        dve.tensor_copy(rkT[:, 2 * (i - 2):2 * (i - 2) + 2, :].rearrange("p h t -> p (h t)"), TURN[i])\
                           .then_inc(rkT_ready, 1)
                    rotate_halves(dve, order, l, 0, z_ga)
                if g == 4:
                    dve.wait_ge(att_turned, 3 * l + 2)
                    dve.tensor_copy(aqT[:, 2:4, :].rearrange("p i t -> p (i t)"), bank[:, 5, :]).then_inc(aqT_second, 1)
                if g == 5:
                    for n in range(T):
                        dve.wait_ge(s_ret_done, 2 * l + n + 1)
                        dve.tensor_tensor(s_ret[:, n, :], bank[:, 3 + n, :], tab("decay"), ALU.mult).then_inc(s_ret_ready, 1)
                if 6 <= g < 6 + PAIRS:
                    n = l * PAIRS + g - 6
                    dve.wait_ge(probs_turned, n + 1)
                    if n:
                        dve.wait_ge(pv_done, n)
                    dve.tensor_copy(probsT[:, 1, :], bank[:, 5, 0:384]).then_inc(probsT_odd, 1)
                if 7 <= g < 7 + PAIRS:
                    i = g - 7
                    dve.wait_ge(oT_hi, l * PAIRS + i + 1)
                    dve.tensor_tensor(uT_lo[:, i, :], bank[:, 3, 0:SEQ], uT_hi[:, i, :].bitcast(F32), ALU.subtract)\
                       .then_inc(oT_lo, 1)
                if 5 <= g < 5 + PAIRS:
                    softmax(l, g - 5)
                if g in (9, 10):
                    retention_out(l, g - 9)

            def gated(c, z, n, t):
                whole(dve, n, t)
                at = slice(c * COLS, (c + 1) * COLS)
                dve.scalar_tensor_tensor(out=z[:, t, at], in0=z[:, t, at], scalar=1.0, in1=OUT[t],
                                         op0=ALU.add, op1=ALU.mult).then_inc(out_free[t], 1)

            def mlp_square(l, f):
                n = l * USES + USE_UP + f
                for b in range(2):
                    m = 2 * (l * F_GROUPS + f) + b
                    dve.wait_ge(out_free[b], n + 1)
                    order.link(dve.tensor_tensor(sq_buf[:, b, :], relu_buf[:, b, :], relu_buf[:, b, :], ALU.mult))
                    dve.wait_ge(up_hi, m + 1)
                    k = (f % 2) * HALF + 2 * b
                    dve.tensor_tensor(uT_lo[:, k:k + 2, :].rearrange("p k t -> p (k t)"), sq_buf[:, b, :],
                                      uT_hi[:, k:k + 2, :].bitcast(F32).rearrange("p k t -> p (k t)"), ALU.subtract)\
                       .then_inc(up_lo, 1)

            for l in range(DEPTH):
                p = l * PIECES
                if l:
                    turn_lo(4 * l, gain=V_MIX + KD * l)
                for t in range(T):
                    row_scale(2 * l, t)
                dve.tensor_scalar(half_rstd[:, l, :], rstd[:, 2 * l, :], 0.5, None, ALU.mult).then_inc(half_ready, 1)
                for g in range(W_IN_GROUPS):
                    if g == 4:
                        window(l, g - 1)
                    step(p + 2 * g)
                    if g != 4:
                        window(l, g - 1)
                    step(p + 2 * g + 1)
                    if g in (RG0, RG1):
                        for t in range(T):
                            dve.wait_ge(tanh_ready, 4 * l + 2 * (g - RG0) + t + 1)
                            dve.scalar_tensor_tensor(out=z_rg[:, t, (g - RG0) * COLS:(g - RG0 + 1) * COLS], in0=rg_tanh[:, t, :],
                                                     scalar=1.0, in1=OUT[t], op0=ALU.add, op1=ALU.mult).then_inc(out_free[t], 1)
                for c in range(2):
                    step(p + PIECE_A + c)
                    for t in range(T):
                        gated(c, z_ga, l * USES + USE_YA + c, t)
                turn_lo(4 * l + 1)
                for c in range(2):
                    step(p + PIECE_B + 2 * c)
                    step(p + PIECE_B + 2 * c + 1)
                    n = l * USES + USE_YB + c
                    for t in range(T):
                        gated(c, z_gb, n, t)
                        dve.wait_ge(out_free[t], n + 1)
                        at = slice(c * COLS, (c + 1) * COLS)
                        dve.tensor_tensor(h[:, t, at], z_ga[:, t, at], z_gb[:, t, at], ALU.add).then_inc(m_ready, 1)
                turn_lo(4 * l + 2, scale=0.5)
                for c in range(2):
                    step(p + PIECE_O + 2 * c)
                    step(p + PIECE_O + 2 * c + 1)
                    for t in range(T):
                        whole(dve, l * USES + USE_O + c, t)
                        at = slice(c * COLS, (c + 1) * COLS)
                        dve.tensor_tensor(x[:, t, at], OUT[t], x[:, t, at], ALU.add).then_inc(out_free[t], 1)
                turn_lo(4 * l + 3, gain=V_MLP + KD * l)
                for t in range(T):
                    row_mean(2 * l + 1, t)
                dve.wait_ge(mean_ready, stat_count(2 * l + 1, T - 1))
                order.link(dve.reciprocal(rstd2[:, l, :], mean[:, 2 * l + 1, :]))
                for f in range(2):
                    step(p + UP_PIECE[f])
                    step(p + UP_PIECE[f] + 1)
                    mlp_square(l, f)
                for f in range(F_GROUPS - 1):
                    step(p + DOWN_PIECE[f])
                    step(p + DOWN_PIECE[f] + 1)
                    if f + 2 < F_GROUPS:
                        step(p + UP_PIECE[f + 2])
                        step(p + UP_PIECE[f + 2] + 1)
                        mlp_square(l, f + 2)
                for c in range(2):
                    if c == 0 or l < DEPTH - 1:
                        step(p + DOWN_PIECE[F_GROUPS - 1] + c)
                    dve.wait_ge(piece_used, p + DOWN_PIECE[F_GROUPS - 1] + c + 1)
                    for t in range(T):
                        at = slice(c * COLS, (c + 1) * COLS)
                        dve.scalar_tensor_tensor(out=x[:, t, at], in0=ACC[t][c], scalar=rstd2[:, l, t:t + 1], in1=x[:, t, at],
                                                 op0=ALU.mult, op1=ALU.add).then_inc(x_mlp, 1)
                        if l == DEPTH - 1:
                            if c == 0 and t == 0:
                                dve.wait_ge(gfinal_landed, 16)
                                dve.wait_ge(s5_angles, 1)
                            dve.wait_ge(x_mlp, 4 * l + 2 * c + t + 1)
                            dve.tensor_tensor(xg[:, t, at], x[:, t, at], g_final[:, at], ALU.mult).then_inc(xg_ready, 1)

            f = 2 * DEPTH
            for t in range(T):
                dve.wait_ge(sq_done[t], 2 * (f + 1) + 2)
                first, second = mean[:, f, t:t + 1], mean[:, f + 1, t:t + 1]
                order.mark(dve.tensor_tensor(second, ssq[:, f + 1, t, 0:1], ssq[:, f + 1, t, 1:2], ALU.add))
                order.link(dve.scalar_tensor_tensor(out=first, in0=ssq[:, f, t, 0:1], scalar=EPS, in1=ssq[:, f, t, 1:2],
                                                    op0=ALU.add, op1=ALU.add))
                order.link(dve.reciprocal(final_inv[:, t:t + 1], first))
                dve.tensor_scalar(second, second, final_inv[:, t:t + 1], EPS, ALU.mult, ALU.add).then_inc(mean_ready, 1)
            for t in range(T):
                dve.wait_ge(rstd_ready, stat_count(f + 1, t))
                for half in range(2):
                    at = slice(half * COLS, (half + 1) * COLS)
                    dve.tensor_scalar(h[:, t, at], xg[:, t, at], rstd[:, f, t:t + 1], rstd[:, f + 1, t:t + 1],
                                      ALU.mult, ALU.mult).then_inc(h_ready, 1)
            split(E_PIECE + 1)
            turn_lo(4 * DEPTH, gain=V_PRE)
            for t in range(T):
                dve.tensor_scalar(x[:, t, :], xg[:, t, :], rstd[:, f, t:t + 1], None, ALU.mult).then_inc(final_scaled, 1)
            dve.memset(pool_in[:, :, 0:POOL_PAD], 0.0).then_inc(pool_zero, 1)

            def rotate_second(g, t):
                dve.wait_ge(out_free[t], E_USE + g + 1)
                half = ROT2 // 2
                z = (zq, zk)[g][:, t, :].rearrange("p (h d) -> p h d", h=ATT2_HEADS)
                z1, z2 = z[:, :, 0:half], z[:, :, half:ROT2]
                cos = tab("att2_cos")[:, t * half:(t + 1) * half].unsqueeze(1).broadcast_to([P, ATT2_HEADS, half])
                sin = tab("att2_sin")[:, t * half:(t + 1) * half].unsqueeze(1).broadcast_to([P, ATT2_HEADS, half])
                r = [rot2_tmp[:, i, :].rearrange("p (h d) -> p h d", h=ATT2_HEADS) for i in range(4)]
                order.mark(dve.tensor_tensor(r[0], z1, cos, ALU.mult))
                order.mark(dve.tensor_tensor(r[1], z2, sin, ALU.mult))
                order.mark(dve.tensor_tensor(r[2], z2, cos, ALU.mult))
                order.mark(dve.tensor_tensor(r[3], z1, sin, ALU.mult))
                order.settle()
                order.mark(dve.tensor_tensor(z1, r[0], r[1], ALU.subtract))
                dve.tensor_tensor(z2, r[2], r[3], ALU.add).then_inc(rope2_done, 1)
                order.settle()
                dve.wait_ge(rope2_done, T * g + t + 1)

            p = E_PIECE
            step(p)
            dve.wait_ge(s5_den, 1)
            dve.reciprocal(s5_small[:, 7, :], s5_small[:, 6, :]).then_inc(s5_inv, 1)
            step(p + 1)
            step(p + 2)
            for t in range(T):
                rotate_second(0, t)
            step(p + 3)
            step(p + 4)
            for t in range(T):
                rotate_second(1, t)
            step(p + 5)
            step(p + 6)
            for i in range(2):
                dve.wait_ge(qk2_turned, i + 3)
                dve.tensor_copy(k2T[:, 2 * i:2 * i + 2, :].rearrange("p h t -> p (h t)"), TURN[2 + i]).then_inc(k2T_ready, 1)
            step(p + 7)
            step(p + 8)
            for hd in range(ATT2_HEADS):
                dve.wait_ge(scores2_done, hd + 1)
                dve.scalar_tensor_tensor(out=probs2[:, hd, :], in0=TURN[hd][:, 0:384], scalar=float(P) ** -0.5,
                                         in1=tab("causal"), op0=ALU.mult, op1=ALU.add).then_inc(scores2_read, 1)
                dve.wait_ge(scores2_read, hd + 1)
                order.mark(dve.tensor_reduce(top2[:, hd, 0:1], probs2[:, hd, 0:P], AX_X, ALU.max))
                order.link(dve.tensor_reduce(top2[:, hd, 1:2], probs2[:, hd, P:3 * P], AX_X, ALU.max))
                dve.tensor_scalar(neg_top2[:, hd, :], top2[:, hd, :], -1.0, None, ALU.mult).then_inc(top2_ready, 1)
            for hd in range(ATT2_HEADS):
                dve.wait_ge(exp2_done, hd + 1)
                order.link(dve.reciprocal(inv_den2[:, hd, :], den2[:, hd, :]))
                for t in range(T):
                    p_at = probs2[:, hd, 0:P] if t == 0 else probs2[:, hd, P:3 * P]
                    last = dve.tensor_scalar(p_at, p_at, inv_den2[:, hd, t:t + 1], None, ALU.mult)
                last.then_inc(probs2_ready, 1)
            step(p + 9)
            step(p + 10)
            for hd in range(2, 4):
                dve.wait_ge(probs2_turned, hd + 1)
                dve.tensor_copy(probs2T[:, hd, :], TURN[hd][:, 0:384]).then_inc(probs2T_dve, 1)

            def cat_lower(count, dst, hi, src):
                dve.wait_ge(cat_hi, count)
                dve.tensor_tensor(dst, src, hi.bitcast(F32), ALU.subtract).then_inc(cat_lo, 1)

            for b in range(2):
                dve.wait_ge(pool_done, b + 1)
                dve.wait_ge(out_free[b], E_USE + 5)
                for j in (2 * b, 2 * b + 1):
                    last = dve.scalar_tensor_tensor(out=mix_tmp[:, HALF + j, :], in0=bank[:, (2, 5)[b], (j % 2) * SEQ:(j % 2 + 1) * SEQ],
                                                    scalar=vec[:, V_PSC + j:V_PSC + j + 1], in1=gate_b[:, j, :],
                                                    op0=ALU.mult, op1=ALU.mult)
                    if j % 2 == 0:
                        order.mark(last)
                last.then_inc(cat_tmp_ready, 1)
            for n, i in enumerate((2, 3)):
                cat_lower(n + 1, uT_lo[:, 2 * i:2 * i + 2, :], uT_hi[:, 2 * i:2 * i + 2, :], mix_tmp[:, 2 * i:2 * i + 2, :])
            step(p + 11)
            for b in range(2):
                dve.wait_ge(pv2_done, 2)
                dve.wait_ge(out_free[b], E_USE + 6)
                dve.tensor_tensor(mix_tmp[:, 2 * b:2 * b + 2, :].rearrange("p k t -> p (k t)"), TURN[b],
                                  gate_a[:, 2 * b:2 * b + 2, :].rearrange("p k t -> p (k t)"), ALU.mult).then_inc(cat_tmp_ready, 1)
            for i in (0, 1):
                cat_lower(2 + i + 1, uT_lo[:, 2 * i:2 * i + 2, :], uT_hi[:, 2 * i:2 * i + 2, :], mix_tmp[:, 2 * i:2 * i + 2, :])

            def step_unless(p, late):
                if p + AHEAD not in late:
                    step(p)

            def post_norm(n, i, use, piece, ready, late=(), between=None):
                for c in range(2):
                    for k in ((0,), (1, 2, 3))[c]:
                        step_unless(piece + k, late)
                    if c == 0:
                        dve.wait_ge(gpost_landed[i], 16)
                    at = slice(c * COLS, (c + 1) * COLS)
                    for t in range(T):
                        dve.wait_ge(sq_done[t], 2 * n + c + 1)
                        dve.tensor_tensor(h[:, t, at], OUT[t], g_post[i][:, at], ALU.mult).then_inc(out_free[t], 1)
                        if c == 0:
                            continue
                        row_mean(n, t)
                        if t and between is not None:
                            between()
                        dve.wait_ge(rstd_ready, stat_count(n, t))
                        dve.wait_ge(out_free[t], use + 2)
                        for half in range(2):
                            to = slice(half * COLS, (half + 1) * COLS)
                            dve.scalar_tensor_tensor(out=x[:, t, to], in0=h[:, t, to], scalar=rstd[:, n, t:t + 1],
                                                     in1=x[:, t, to], op0=ALU.mult, op1=ALU.add).then_inc(ready, 1)

            post_norm(2 * DEPTH + 2, 0, E_OUT_USE, E_OUT_PIECE, post_ready, late=(O_PIECE + 1,),
                      between=lambda: row_mean(2 * DEPTH + 3, 0))
            for t in range(T):
                if t:
                    row_mean(2 * DEPTH + 3, t)
                dve.wait_ge(rstd_ready, stat_count(2 * DEPTH + 3, t))
                for half in range(2):
                    at = slice(half * COLS, (half + 1) * COLS)
                    dve.tensor_scalar(h[:, t, at], x[:, t, at], rstd[:, 2 * DEPTH + 3, t:t + 1], None, ALU.mult)\
                       .then_inc(h_ready, 1)
            turn_lo(4 * DEPTH + 1, gain=V_PRE + KD)
            split(O_PIECE + 1)
            p = O_PIECE
            dve.memset(conv_in[:, :, 0:CONV_K - 1], 0.0).then_inc(conv_zero, 1)
            dve.wait_ge(s5_tables, 2)
            dve.wait_ge(s5_mats, 5)

            def turn_back(j):
                dve.wait_ge(drive_done, j + 1)
                if j >= 2:
                    dve.wait_ge(y_done, j - 1)
                re, im = bank[:, 4:8, 0:SEQ], bank[:, 4:8, SEQ:2 * SEQ]
                cos, sin = s5_cos[:, 4 * j:4 * j + 4, :], s5_sin[:, 4 * j:4 * j + 4, :]
                x_re, x_im = s5_x[j % 2]
                part = s5_part[:, :, :]
                order.mark(dve.tensor_tensor(x_re, re, cos, ALU.mult))
                order.mark(dve.tensor_tensor(part, im, sin, ALU.mult))
                order.mark(dve.tensor_tensor(x_im, im, cos, ALU.mult))
                order.settle()
                order.link(dve.tensor_tensor(x_re, x_re, part, ALU.add))
                dve.tensor_tensor(part, re, sin, ALU.mult).then_inc(drive_read, 1)
                dve.wait_ge(drive_read, j + 1)
                order.link(dve.tensor_tensor(x_im, x_im, part, ALU.subtract))

            def scan(j):
                for q in range(4):
                    decay = s5_small[:, 2, 4 * j + q:4 * j + q + 1].broadcast_to([P, SEQ])
                    for v in s5_x[j % 2]:
                        last = dve.tensor_tensor_scan(v[:, q, :], decay, v[:, q, :], 0.0, ALU.mult, ALU.add)
                last.then_inc(scans_done, 1)

            def convolve(k0, k1):
                blocks = HALF - PE_CONV
                for k in range(k0, k1):
                    for b in range(blocks):
                        j = PE_CONV + b
                        src, w = conv_in[:, j, k:k + SEQ], conv_w[:, k, j:j + 1]
                        if k == 0:
                            dve.wait_ge(conv_gated, 1)
                            order.mark(dve.tensor_scalar(conv_out[:, j, :], src, w, None, ALU.mult))
                            step_mark[b] = order.n
                            continue
                        dve.wait_ge(dve_order, step_mark[b])
                        ins_ = dve.scalar_tensor_tensor(out=conv_out[:, j, :], in0=src, scalar=w, in1=conv_out[:, j, :],
                                                        op0=ALU.mult, op1=ALU.add)
                        if k < CONV_K - 1:
                            order.mark(ins_)
                            step_mark[b] = order.n
                        else:
                            ins_.then_inc(conv_done, 1)

            step_mark = {}

            def outputs(j):
                dve.wait_ge(y_done, j + 1)
                dve.scalar_tensor_tensor(out=y_ssm[:, j, :], in0=su[:, j, :], scalar=vec[:, V_D + j:V_D + j + 1],
                                         in1=bank[:, 2, 0:SEQ], op0=ALU.mult, op1=ALU.add).then_inc(y_ready, 1)

            for i in range(3):
                step(p + i)
            turn_back(0)
            step(p + 3)
            scan(0)
            step(p + 4)
            turn_back(1)
            step(p + 5)
            scan(1)
            step(p + 6)
            convolve(0, 5)
            outputs(0)
            turn_back(2)
            step(p + 7)
            scan(2)
            step(p + 8)
            step(p + 9)
            outputs(1)
            turn_back(3)
            step(GLU_PIECE)
            scan(3)
            outputs(2)
            convolve(5, 27)
            outputs(3)
            convolve(27, CONV_K)
            for t in range(T):
                dve.wait_ge(conv_turned, t + 1)
                order.link(dve.bn_stats(ln_stat[:, t, :], bank[:, 4 + t, :]))
                order.link(dve.bn_aggr(ln_mv[:, t, :], ln_stat[:, t, :]))
            dve.tensor_scalar(ln_var[:, :], ln_mv[:, :, 1], EPS, None, ALU.add).then_inc(ln_var_ready, 1)
            dve.wait_ge(ln_scale, 1)
            for t in range(T):
                dve.tensor_scalar(conv_tok[:, t, :], bank[:, 4 + t, :], ln_mv[:, t, 0:1], ln_rstd[:, t:t + 1],
                                  ALU.subtract, ALU.mult).then_inc(ln_done, 1)
            for b in range(2):
                whole(dve, GLU_USE, b)
                for j in (2 * b, 2 * b + 1):
                    last = dve.scalar_tensor_tensor(out=glu_a[:, j, :], in0=OUT[b][:, (j % 2) * SEQ:(j % 2 + 1) * SEQ],
                                                    scalar=vec[:, V_GLUB + j:V_GLUB + j + 1], in1=gate_c[:, j, :],
                                                    op0=ALU.add, op1=ALU.mult)
                last.then_inc(out_free[b], 1)
            step(GLU_PIECE + 1)
            for b in range(2):
                at = slice(HALF + 2 * b, HALF + 2 * b + 2)
                dve.wait_ge(cat_hi, 8 + b + 1)
                dve.tensor_tensor(hT_lo[:, at, :], conv_act[:, 2 * b:2 * b + 2, :], hT_hi[:, at, :].bitcast(F32), ALU.subtract)\
                   .then_inc(cat_lo, 1)
            step(PW_PIECE)
            for b in range(2):
                dve.wait_ge(out_free[b], GLU_USE + 2)
                at = slice(2 * b, 2 * b + 2)
                dve.tensor_tensor(cat_tmp[:, at, :], glu_a[:, at, :], glu_s[:, at, :], ALU.mult).then_inc(cat_tmp_ready, 1)
            for i in range(2):
                cat_lower(8 + 2 + i + 1, uT_lo[:, 2 * i:2 * i + 2, :], uT_hi[:, 2 * i:2 * i + 2, :], cat_tmp[:, 2 * i:2 * i + 2, :])
            for b in range(2):
                whole(dve, PW_USE, b)
                at = slice(2 * b, 2 * b + 2)
                dve.tensor_tensor(cat_tmp[:, HALF + 2 * b:HALF + 2 * b + 2, :].rearrange("p k t -> p (k t)"), PW_BANKS[b],
                                  gate_d[:, at, :].rearrange("p k t -> p (k t)"), ALU.mult).then_inc(out_free[b], 1)
            for i in range(2, 4):
                cat_lower(8 + 2 + i + 1, uT_lo[:, 2 * i:2 * i + 2, :], uT_hi[:, 2 * i:2 * i + 2, :], cat_tmp[:, 2 * i:2 * i + 2, :])
            post_norm(2 * DEPTH + 4, 1, O_OUT_USE, O_OUT_PIECE, x_final)

        @block.gpsimd
        def _(pool):
            order = Order(pool, pool_order)

            def inverse_root(dst, src, n, done):
                pool.tensor_tensor(dst, src, tab("minus_half")[:, 0:n], ALU.pow).then_inc(done, 1)

            def row_scale(n):
                for t in range(T):
                    pool.wait_ge(mean_ready, stat_count(n, t))
                    if n == 2 * DEPTH:
                        inverse_root(rstd[:, n:n + 2, t], mean[:, n:n + 2, t], 2, rstd_ready)
                    else:
                        inverse_root(rstd[:, n, t:t + 1], mean[:, n, t:t + 1], 1, rstd_ready)

            def turns_left(v):
                order.link(pool.tensor_scalar(s5_tmp, v, ROUND, -ROUND, ALU.add, ALU.add))
                order.link(pool.tensor_tensor(v, v, s5_tmp, ALU.subtract))

            def state_space_angles():
                pool.wait_ge(out_free[1], (DEPTH - 1) * USES + USE_UP)
                lam_re, lam_im = vec[:, V_LRE:V_LRE + S5_TILES], vec[:, V_LIM:V_LIM + S5_TILES]
                s = [s5_small[:, i, :] for i in range(16)]
                pool.tensor_tensor(s[0], lam_re, s5_dt[:, :], ALU.mult).then_inc(s5_decay_in, 1)
                order.mark(pool.tensor_tensor(s[1], lam_im, s5_dt[:, :], ALU.mult))
                order.mark(pool.tensor_tensor(s[5], lam_re, lam_re, ALU.mult))
                order.link(pool.tensor_tensor(s[13], lam_im, lam_im, ALU.mult))
                pool.tensor_tensor(s[6], s[5], s[13], ALU.add).then_inc(s5_den, 1)
                order.link(pool.tensor_scalar(s[1], s[1], TO_TURNS, None, ALU.mult))
                order.link(pool.tensor_scalar(s[3], s[1], 4097.0, None, ALU.mult))
                order.link(pool.tensor_tensor(s[4], s[3], s[1], ALU.subtract))
                order.link(pool.tensor_tensor(s[3], s[3], s[4], ALU.subtract))
                order.link(pool.tensor_tensor(s[4], s[1], s[3], ALU.subtract))
                for i in range(S5_TILES):
                    order.mark(pool.tensor_scalar(s5_sin[:, i, :], tab("time"), s5_small[:, 3, i:i + 1], None, ALU.mult))
                order.settle()
                turns_left(s5_sin)
                for i in range(S5_TILES):
                    order.mark(pool.tensor_scalar(s5_cos[:, i, :], tab("time"), s5_small[:, 4, i:i + 1], None, ALU.mult))
                order.settle()
                order.link(pool.tensor_tensor(s5_sin, s5_sin, s5_cos, ALU.add))
                turns_left(s5_sin)
                order.link(pool.tensor_scalar(s5_cos, s5_sin, 0.25, None, ALU.add))
                order.link(pool.tensor_scalar(s5_tmp, s5_cos, ROUND, -ROUND, ALU.add, ALU.add))
                pool.tensor_tensor(s5_cos, s5_cos, s5_tmp, ALU.subtract).then_inc(s5_angles, 1)

            def pool_means():
                pool.wait_ge(pool_zero, 1)
                for b in range(2):
                    pool.wait_ge(out_free[b], E_USE + 4)
                pool.wait_ge(qk2_turned, 4)
                order.link(pool.tensor_tensor(pool_s1[:, :, 1:PW], pool_in[:, :, 1:PW], pool_in[:, :, 0:PW - 1], ALU.add))
                order.link(pool.tensor_tensor(pool_s2[:, :, 3:PW], pool_s1[:, 1:4, 3:PW], pool_s1[:, 1:4, 1:PW - 2], ALU.add))
                order.link(pool.tensor_tensor(pool_s1[:, 2:4, 7:PW], pool_s2[:, 1:3, 7:PW], pool_s2[:, 1:3, 3:PW - 4], ALU.add))
                order.link(pool.tensor_tensor(pool_s2[:, 2, 15:PW], pool_s1[:, 3, 15:PW], pool_s1[:, 3, 7:PW - 8], ALU.add))
                pool.wait_ge(piece_used, E_PIECE)
                for g, w in enumerate(POOL_WINDOWS):
                    win = (pool_s1[:, 0, :], pool_s2[:, 0, :], pool_s1[:, 2, :], pool_s2[:, 2, :])[g]
                    first = tab("pool_first")[:, g * POOL_PAD:(g + 1) * POOL_PAD]
                    at, late = slice(POOL_PAD, 2 * POOL_PAD), slice(2 * POOL_PAD, PW)
                    order.mark(pool.tensor_scalar(pool_m[:, g, POOL_PAD:SEQ], win[:, late], 1.0 / w, None, ALU.mult))
                    order.mark(pool.tensor_tensor(pool_m[:, g, 0:POOL_PAD], win[:, at], first, ALU.mult))
                order.settle()
                pool.tensor_tensor(pool_m[:, :, :], pool_m[:, :, :], pool_in[:, :, POOL_PAD:PW], ALU.subtract).then_inc(pool_mean, 1)
                pool.wait_ge(pool_mean, 1)

            def state_space_matrices():
                pool.wait_ge(s5_tables, 2)
                pool.wait_ge(s5_decay, 1)
                pool.wait_ge(s5_inv, 1)
                pool.wait_ge(s5_landed, 16 * 4)
                lam_re, lam_im = vec[:, V_LRE:V_LRE + S5_TILES], vec[:, V_LIM:V_LIM + S5_TILES]
                s = [s5_small[:, i, :] for i in range(16)]
                order.mark(pool.tensor_tensor(s[8], s[2], s5_cos[:, :, 1], ALU.mult))
                order.link(pool.tensor_tensor(s[9], s[2], s5_sin[:, :, 1], ALU.mult))
                order.link(pool.tensor_scalar(s[8], s[8], -1.0, None, ALU.add))
                order.mark(pool.tensor_tensor(s[10], s[8], lam_re, ALU.mult))
                order.mark(pool.tensor_tensor(s[11], s[9], lam_im, ALU.mult))
                order.mark(pool.tensor_tensor(s[12], s[9], lam_re, ALU.mult))
                order.link(pool.tensor_tensor(s[13], s[8], lam_im, ALU.mult))
                order.mark(pool.tensor_tensor(s[10], s[10], s[11], ALU.add))
                order.link(pool.tensor_tensor(s[12], s[12], s[13], ALU.subtract))
                order.mark(pool.tensor_tensor(s[10], s[10], s[7], ALU.mult))
                order.link(pool.tensor_tensor(s[12], s[12], s[7], ALU.mult))
                f_re, f_im = (v.unsqueeze(2).broadcast_to([P, S5_TILES, S5_IN]) for v in (s[10], s[12]))
                for i, (v, b) in enumerate(((f_re, 0), (f_im, 1), (f_re, 1), (f_im, 0))):
                    order.mark(pool.tensor_tensor(b_bar[:, i, :, :], v, b_in[:, b, :, :], ALU.mult))
                order.settle()
                order.mark(pool.tensor_tensor(b_bar[:, 0, :, :], b_bar[:, 0, :, :], b_bar[:, 1, :, :], ALU.subtract))
                order.link(pool.tensor_tensor(b_bar[:, 2, :, :], b_bar[:, 2, :, :], b_bar[:, 3, :, :], ALU.add))
                for b in range(2):
                    for g in range(2):
                        pool.tensor_scalar(b_pad[:, b, :, g * S5_IN:(g + 1) * S5_IN], b_bar[:, 2 * b, :, :],
                                           tab("odd_group_state")[:, g:g + 1], None, ALU.mult).then_inc(s5_padded, 1)
                        pool.tensor_scalar(c_pad[:, b, :, g * S5_STATE:(g + 1) * S5_STATE], c_in[:, b, :, :],
                                           tab("odd_group_row")[:, g:g + 1], None, ALU.mult).then_inc(s5_padded, 1)

            def conv_diagonals():
                pool.wait_ge(scores2_read, ATT2_HEADS)
                for chunk in range(2):
                    at = slice(chunk * CHUNK, (chunk + 1) * CHUNK)
                    pool.tensor_tensor(conv_diag[:, at, :], ident.unsqueeze(1).broadcast_to([P, CHUNK, P]),
                                       conv_w[:, at, 0].unsqueeze(2).broadcast_to([P, CHUNK, P]), ALU.mult)\
                        .then_inc(conv_diag_ready, 1)

            def gate_conv():
                for b in range(2):
                    pool.wait_ge(out_free[b], O_USE + CB + 1)
                c_at = conv_in[:, :, CONV_K - 1:CW]
                pool.tensor_tensor(c_at, c_at, gate_d[:, :, :], ALU.mult).then_inc(conv_gated, 1)

            def turn_states(j):
                pool.wait_ge(scans_done, j + 1)
                if j:
                    pool.wait_ge(y_done, j)
                cos, sin = s5_cos[:, 4 * j:4 * j + 4, :], s5_sin[:, 4 * j:4 * j + 4, :]
                for v, o in zip(s5_x[j % 2], s5_o):
                    order.mark(pool.tensor_tensor(o, v, sin, ALU.mult))
                order.settle()
                for i, v in enumerate(s5_x[j % 2]):
                    last = pool.tensor_tensor(v, v, cos, ALU.mult)
                    if i == 0:
                        order.mark(last)
                last.then_inc(states_ready, 1)

            pool.wait_ge(ident_landed, 16)
            row_scale(0)
            pool.wait_ge(const_landed, 16)
            pool.wait_ge(vec_ready, 4)
            for l in range(DEPTH):
                rotate_pairs(pool, order, l, 1, z_gb)
                pool.wait_ge(rot_done[0], l + 1)
                zeta = tab("zeta").unsqueeze(2).broadcast_to([P, RET_HEADS, RET_QK])
                pool.tensor_tensor(rk_zeta.rearrange("p (h d) -> p h d", h=RET_HEADS),
                                   z_ret[:, 0, 512:1024].rearrange("p (h d) -> p h d", h=RET_HEADS), zeta, ALU.mult)\
                    .then_inc(rkz_ready, 1)
                rotate_halves(pool, order, l, 1, z_gb)
                pool.wait_ge(rqT_ready, 2 * l + 2)
                pool.tensor_tensor(rqT_xi[:, :, :], rqT[:, :, P:SEQ], tab("xi").rearrange("p (h i) -> p h i", h=RET_HEADS),
                                   ALU.mult).then_inc(rqxi_ready, 1)
                for t in range(T):
                    pool.wait_ge(ret_mean, 2 * l + t + 1)
                    order.link(pool.tensor_tensor(ret_rstd[:, t, :], ret_ms[:, t, :], tab("minus_half")[:, 0:RET_HEADS], ALU.pow))
                    pool.tensor_scalar(ret_rstd[:, t, :], ret_rstd[:, t, :], rstd[:, 2 * l, t:t + 1], None, ALU.mult)\
                        .then_inc(ret_scale, 1)
                row_scale(2 * l + 1)
                if l == DEPTH - 1:
                    state_space_angles()
                row_scale(2 * l + 2)
            pool_means()
            state_space_matrices()
            conv_diagonals()
            row_scale(2 * DEPTH + 2)
            row_scale(2 * DEPTH + 3)
            def split(p):
                pool.wait_ge(hi_ready, p + 1)
                pool.tensor_tensor(w_lo[:, p % SPLIT_RING, :, :], raw[:, p % RAW_RING, :, :],
                                   w_hi[:, p % SPLIT_RING, :, :].bitcast(F32), ALU.subtract).then_inc(lo_pool_ready, 1)

            for j in range(HALF):
                if j == 1:
                    gate_conv()
                if j == HALF - 1:
                    for p in POOL_PIECES[:2]:
                        split(p)
                turn_states(j)
            for j in range(HALF):
                pool.wait_ge(cat_hi, 4 + j + 1)
                pool.tensor_tensor(hT_lo[:, j, :], y_ssm[:, j, :], hT_hi[:, j, :].bitcast(F32), ALU.subtract).then_inc(y_lo, 1)
            pool.wait_ge(ln_var_ready, 1)
            inverse_root(ln_rstd[:, :], ln_var[:, :], T, ln_scale)
            for p in POOL_PIECES[2:]:
                split(p)
            row_scale(2 * DEPTH + 4)


OUT_SHAPE = (1, SEQ, D)


def kernel(**inputs):
    import concourse.bacc as bacc
    from concourse.bass_utils import run_bass_kernel_spmd

    nc = bacc.Bacc("TRN2", target_bir_lowering=False, num_devices=1)
    arrays, ins = {}, {}
    for name in inputs:
        a = np.ascontiguousarray(inputs[name])
        arrays[f"in_{name}"] = a
        ins[name] = nc.dram_tensor(f"in_{name}", a.shape, mybir.dt.from_np(a.dtype), kind="ExternalInput").ap()
    tables, where = shape_constants()
    arrays["shape_tables"] = tables
    consts = nc.dram_tensor("shape_tables", tables.shape, F32, kind="ExternalInput").ap()
    out = nc.dram_tensor("out_0", OUT_SHAPE, F32, kind="ExternalOutput").ap()
    build_program(nc, ins, consts, where, out)
    r = run_bass_kernel_spmd(nc, [arrays], core_ids=[0])
    return r.results[0]["out_0"]
```
